# Optimizing a Trainium2 kernel written in Bass

```python
import math
import jax, jax.numpy as jnp
from jax import lax
import numpy as np

D_MODEL = 1024
BATCH = 1
SEQ = 512
DEPTH = 1

CHUNK = 64
Q_BLOCK = 128
EPS = 1e-6
H_A = 4
DH_A = 64
W_A = H_A * 2 * DH_A
H_B = 8
DH_B = 64
W_B = H_B * DH_B
H_I = 4
D_I = 64
TOPK_MAX = 256
N_MEM = 256
H_X = 4
DH_X = D_MODEL // H_X
N_GROUPS = 4
EXP_PER_GROUP = 8
N_EXPERTS = N_GROUPS * EXP_PER_GROUP
TOP_K_INNER = 2
D_EXPERT = 512
MOE_BLOCK = 256

IN_WIDTHS = (H_A * 2 * DH_A, H_A * 2 * DH_A, H_A * 2 * DH_A, H_B * DH_B, DH_B, DH_B, H_I * D_I, D_I, H_I)
D_IN = sum(IN_WIDTHS)
IN_SPLITS = tuple(sum(IN_WIDTHS[:i + 1]) for i in range(len(IN_WIDTHS) - 1))

kernel_name = "hybrid_diff_dsa_hiermoe_block"

def rms_norm(x, g):
    xf = x.astype(jnp.float32)
    y = xf * lax.rsqrt(jnp.mean(xf * xf, axis=-1, keepdims=True) + EPS)
    return (y * g.astype(jnp.float32)).astype(x.dtype)

def alibi_slopes(n):
    return jnp.asarray([2.0 ** (-8.0 * (i + 1) / n) for i in range(n)], dtype=jnp.float32)

def to_blocks(a):
    b, s = a.shape[:2]
    a = a.reshape((b, s // Q_BLOCK, Q_BLOCK) + a.shape[2:])
    return jnp.moveaxis(a, 1, 0)

def from_blocks(o):
    o = jnp.moveaxis(o, 0, 1)
    return o.reshape((o.shape[0], o.shape[1] * o.shape[2]) + o.shape[3:])

def chunk_allowed(t, s):
    return (t[:, None] // CHUNK) >= (s[None, :] // CHUNK)

def diff_attention(q, k, v, lam, slopes):
    s_len = q.shape[1]
    pos = jnp.arange(s_len, dtype=jnp.int32)
    scale = DH_A ** -0.5

    def one_block(args):
        q_blk, t = args
        sc = jnp.einsum('bqhmd,bshmd->bhmqs', q_blk, k).astype(jnp.float32) * scale
        dist = jnp.abs(t[:, None] - pos[None, :]).astype(jnp.float32)
        sc = sc - slopes[None, :, None, None, None] * dist
        sc = jnp.where(chunk_allowed(t, pos), sc, -jnp.inf)
        p = jax.nn.softmax(sc, axis=-1)
        a = p[:, :, 0] - lam * p[:, :, 1]
        return jnp.einsum('bhqs,bshe->bqhe', a.astype(v.dtype), v)

    o = lax.map(one_block, (to_blocks(q), pos.reshape(-1, Q_BLOCK)))
    return from_blocks(o)

def dsa_attention(q, k, v, q_idx, k_idx, w_idx, slopes, k_sel):
    s_len = q.shape[1]
    pos = jnp.arange(s_len, dtype=jnp.int32)
    scale = DH_B ** -0.5
    gather = jax.vmap(lambda arr, ii: arr[ii])

    def one_block(args):
        q_blk, qi_blk, wi_blk, t = args
        dots = jnp.einsum('bqhd,bsd->bqhs', qi_blk, k_idx).astype(jnp.float32)
        isc = jnp.einsum('bqhs,bqh->bqs', jax.nn.relu(dots), wi_blk.astype(jnp.float32))
        isc = jnp.where(chunk_allowed(t, pos)[None], isc, -jnp.inf)
        top_val, top_idx = lax.top_k(isc, k_sel)
        valid = top_val > -jnp.inf
        k_g = gather(k, top_idx)
        v_g = gather(v, top_idx)
        sc = jnp.einsum('bqhd,bqkd->bhqk', q_blk, k_g).astype(jnp.float32) * scale
        dist = jnp.abs(t[None, :, None] - top_idx).astype(jnp.float32)
        sc = sc - slopes[None, :, None, None] * dist[:, None]
        sc = jnp.where(valid[:, None], sc, -jnp.inf)
        p = jax.nn.softmax(sc, axis=-1)
        return jnp.einsum('bhqk,bqkd->bqhd', p.astype(v.dtype), v_g)

    o = lax.map(one_block, (to_blocks(q), to_blocks(q_idx), to_blocks(w_idx), pos.reshape(-1, Q_BLOCK)))
    return from_blocks(o)

def memory_cross_attention(xn, memn, w_cq, w_ckv, w_co):
    b, s, d = xn.shape
    m = memn.shape[1]
    q = (xn @ w_cq).reshape(b, s, H_X, DH_X)
    k, v = jnp.split((memn @ w_ckv).reshape(m and b, m, 2, H_X, DH_X), 2, axis=2)
    k, v = k[:, :, 0], v[:, :, 0]
    sc = jnp.einsum('bshd,bmhd->bhsm', q, k).astype(jnp.float32) * (DH_X ** -0.5)
    p = jax.nn.softmax(sc, axis=-1)
    o = jnp.einsum('bhsm,bmhd->bshd', p.astype(v.dtype), v).reshape(b, s, d)
    return o @ w_co

def hier_moe(x2, w_group, b_group, w_router, b_router, w1, w3, w2):
    n, d = x2.shape
    g_logits = (x2 @ w_group).astype(jnp.float32) + b_group.astype(jnp.float32)
    p_group = jax.nn.softmax(g_logits, axis=-1)
    g_idx = jnp.argmax(g_logits, axis=-1).astype(jnp.int32)
    p_g = jnp.take_along_axis(p_group, g_idx[:, None], axis=1)[:, 0]
    e_logits = ((x2 @ w_router).astype(jnp.float32) + b_router.astype(jnp.float32)).reshape(n, N_GROUPS, EXP_PER_GROUP)
    e_in = jnp.take_along_axis(e_logits, g_idx[:, None, None], axis=1)[:, 0]
    top_p, top_i = lax.top_k(jax.nn.softmax(e_in, axis=-1), TOP_K_INNER)
    gate = p_g[:, None] * top_p / jnp.sum(top_p, axis=-1, keepdims=True)
    expert = g_idx[:, None] * EXP_PER_GROUP + top_i.astype(jnp.int32)

    flat_e = expert.reshape(-1)
    n_assign = flat_e.shape[0]
    flat_tok = jnp.repeat(jnp.arange(n, dtype=jnp.int32), TOP_K_INNER)
    flat_gate = gate.reshape(-1)
    order = jnp.argsort(flat_e)
    sorted_e = flat_e[order]
    counts = jnp.bincount(flat_e, length=N_EXPERTS).astype(jnp.int32)
    padded = (counts + MOE_BLOCK - 1) // MOE_BLOCK * MOE_BLOCK
    pad_end = jnp.cumsum(padded)
    pad_start = pad_end - padded
    start = jnp.cumsum(counts) - counts
    rank = jnp.arange(n_assign, dtype=jnp.int32) - start[sorted_e]
    dest = pad_start[sorted_e] + rank
    n_blocks = -(-n_assign // MOE_BLOCK) + N_EXPERTS
    n_slots = n_blocks * MOE_BLOCK
    slot_tok = jnp.full((n_slots,), n, dtype=jnp.int32).at[dest].set(flat_tok[order])
    slot_gate = jnp.zeros((n_slots,), jnp.float32).at[dest].set(flat_gate[order])
    block_expert = jnp.minimum(
        jnp.searchsorted(pad_end, jnp.arange(n_blocks, dtype=jnp.int32) * MOE_BLOCK, side='right'),
        N_EXPERTS - 1).astype(jnp.int32)
    x_pad = jnp.concatenate([x2, jnp.zeros((1, d), x2.dtype)], axis=0)

    def expert_block(args):
        tok, gte, e = args
        xb = x_pad[tok]
        hb = jax.nn.silu(xb @ w1[e]) * (xb @ w3[e])
        return (hb @ w2[e]) * gte[:, None].astype(x2.dtype)

    y_slots = lax.map(expert_block, (slot_tok.reshape(n_blocks, MOE_BLOCK),
                                     slot_gate.reshape(n_blocks, MOE_BLOCK), block_expert))
    y = jnp.zeros((n + 1, d), x2.dtype).at[slot_tok].add(y_slots.reshape(n_slots, d))
    return y[:n]

def setup_inputs(seed: int = 0) -> dict:
    key = jax.random.key(seed)
    ks = jax.random.split(key, 32)

    def nrm(k, shape, scale):
        return jax.random.normal(k, shape, jnp.float32) * scale

    def gain(k, shape):
        return 1.0 + 0.02 * jax.random.normal(k, shape, jnp.float32)

    L, D = DEPTH, D_MODEL
    return {
        "x": nrm(ks[0], (BATCH, SEQ, D), 1.0),
        "mem": nrm(ks[1], (BATCH, N_MEM, D), 1.0),
        "mix_norm": gain(ks[2], (L, D)),
        "w_in": nrm(ks[3], (L, D, D_IN), D ** -0.5),
        "lam_q1": nrm(ks[4], (L, DH_A), 0.1),
        "lam_k1": nrm(ks[5], (L, DH_A), 0.1),
        "lam_q2": nrm(ks[6], (L, DH_A), 0.1),
        "lam_k2": nrm(ks[7], (L, DH_A), 0.1),
        "diff_subln": gain(ks[8], (L, 2 * DH_A)),
        "w_branch_a": nrm(ks[9], (L, W_A, D), W_A ** -0.5),
        "w_branch_b": nrm(ks[10], (L, W_B, D), W_B ** -0.5),
        "w_gate": nrm(ks[11], (L, D, 2 * D), D ** -0.5),
        "b_gate": nrm(ks[12], (L, 2 * D), 0.02),
        "w_out": nrm(ks[13], (L, D, D), D ** -0.5),
        "cross_norm": gain(ks[14], (L, D)),
        "mem_norm": gain(ks[15], (L, D)),
        "w_cq": nrm(ks[16], (L, D, D), D ** -0.5),
        "w_ckv": nrm(ks[17], (L, D, 2 * D), D ** -0.5),
        "w_co": nrm(ks[18], (L, D, D), D ** -0.5),
        "ffn_norm": gain(ks[19], (L, D)),
        "w_group": nrm(ks[20], (L, D, N_GROUPS), D ** -0.5),
        "b_group": nrm(ks[21], (L, N_GROUPS), 0.01),
        "w_router": nrm(ks[22], (L, D, N_EXPERTS), D ** -0.5),
        "b_router": nrm(ks[23], (L, N_EXPERTS), 0.01),
        "w1": nrm(ks[24], (L, N_EXPERTS, D, D_EXPERT), D ** -0.5),
        "w3": nrm(ks[25], (L, N_EXPERTS, D, D_EXPERT), D ** -0.5),
        "w2": nrm(ks[26], (L, N_EXPERTS, D_EXPERT, D), D_EXPERT ** -0.5),
        "final_norm": gain(ks[27], (D,)),
    }

def reference(x, mem, mix_norm, w_in, lam_q1, lam_k1, lam_q2, lam_k2, diff_subln, w_branch_a, w_branch_b,
              w_gate, b_gate, w_out, cross_norm, mem_norm, w_cq, w_ckv, w_co, ffn_norm, w_group, b_group,
              w_router, b_router, w1, w3, w2, final_norm):
    b, s, d = x.shape
    k_sel = min(TOPK_MAX, s // 4)
    slopes_a = alibi_slopes(H_A)
    slopes_b = alibi_slopes(H_B)
    h = x
    for l in range(DEPTH):
        lambda_init = 0.8 - 0.6 * math.exp(-0.3 * l)
        xn = rms_norm(h, mix_norm[l])
        q_a, k_a, v_a, q_b, k_b, v_b, q_i, k_i, w_i = jnp.split(xn @ w_in[l], IN_SPLITS, axis=-1)
        lam = (jnp.exp(jnp.sum(lam_q1[l].astype(jnp.float32) * lam_k1[l].astype(jnp.float32)))
               - jnp.exp(jnp.sum(lam_q2[l].astype(jnp.float32) * lam_k2[l].astype(jnp.float32)))
               + lambda_init)
        y_a = diff_attention(q_a.reshape(b, s, H_A, 2, DH_A), k_a.reshape(b, s, H_A, 2, DH_A),
                             v_a.reshape(b, s, H_A, 2 * DH_A), lam, slopes_a)
        y_a = (rms_norm(y_a, diff_subln[l]) * (1.0 - lambda_init)).reshape(b, s, W_A)
        y_b = dsa_attention(q_b.reshape(b, s, H_B, DH_B), k_b, v_b,
                            q_i.reshape(b, s, H_I, D_I), k_i,
                            w_i * (H_I ** -0.5 * D_I ** -0.5), slopes_b, k_sel).reshape(b, s, W_B)
        gates = jax.nn.sigmoid((xn @ w_gate[l]).astype(jnp.float32) + b_gate[l].astype(jnp.float32)).astype(h.dtype)
        g_a, g_b = jnp.split(gates, 2, axis=-1)
        merged = g_a * (y_a @ w_branch_a[l]) + g_b * (y_b @ w_branch_b[l])
        h = h + merged @ w_out[l]
        h = h + memory_cross_attention(rms_norm(h, cross_norm[l]), rms_norm(mem, mem_norm[l]),
                                       w_cq[l], w_ckv[l], w_co[l])
        y_f = hier_moe(rms_norm(h, ffn_norm[l]).reshape(b * s, d), w_group[l], b_group[l],
                       w_router[l], b_router[l], w1[l], w3[l], w2[l])
        h = h + y_f.reshape(b, s, d)
    return rms_norm(h, final_norm)


_drawn_inputs = setup_inputs


def setup_inputs(seed=0):
    import zlib

    import numpy as np

    out = dict(_drawn_inputs(seed))
    spreads = {}
    factors = {'lam_q2': 2.759,
     'b_gate': 4.429,
     'cross_norm': 6.169,
     'mem_norm': 8.0,
     'b_group': 56.736,
     'b_router': 33.808,
     'final_norm': 9.706,
     'ffn_norm': 8.0}
    for name, (base, spread) in spreads.items():
        noise = np.random.default_rng([zlib.crc32(name.encode()), seed]).standard_normal(out[name].shape)
        drawn = base * np.exp(spread * noise) if base else spread * noise
        out[name] = __import__('jax').numpy.asarray(drawn.astype(out[name].dtype))
    for name, factor in factors.items():
        out[name] = (out[name] * factor).astype(out[name].dtype)
    return out
```

```python
import math

import concourse.bass as bass
from concourse import mybir

EPS = 1e-6
D = 1024
SEQ = 512
P = 128
KT = D // P
TT = SEQ // P
CHUNK = 64
H_A, DH_A = 4, 64
H_B, DH_B = 8, 64
H_I, D_I = 4, 64
K_SEL = min(256, SEQ // 4)
N_MEM = 256
MT = N_MEM // P
H_X = 4
DH_X = D // H_X
NG, EPG = 4, 8
NE = NG * EPG
DE = 512
BLK = 64
TOPK = 2
MAX_OVER = SEQ * TOPK // (BLK + 1) + 1
N_BLOCKS = -(-(NE + MAX_OVER + 1) // 2) * 2
LAMBDA_INIT = 0.8 - 0.6 * math.exp(-0.3 * 0)
BIG = 1e30
TAKEN = -3e38
NROUND = K_SEL // 8

C_QA, C_KA, C_VA = 0, 512, 1024
C_QB, C_KB, C_VB = 1536, 2048, 2112
C_QI, C_KI, C_WI = 2176, 2432, 2496


def build(nc, x, mem, mix_norm, w_in, lam_q1, lam_k1, lam_q2, lam_k2, diff_subln, w_branch_a, w_branch_b,
          w_gate, b_gate, w_out, cross_norm, mem_norm, w_cq, w_ckv, w_co, ffn_norm, w_group, b_group,
          w_router, b_router, w1, w3, w2, final_norm, out):
    f32, f32r, bf16, i32 = mybir.dt.float32, mybir.dt.float32r, mybir.dt.bfloat16, mybir.dt.int32
    ACT, ALU, AX = mybir.ActivationFunctionType, mybir.AluOpType, mybir.AxisListType

    sbuf_at = [-(-nc.sbuf_base // 32) * 32]

    def region(nbytes):
        start = sbuf_at[0]
        sbuf_at[0] += -(-nbytes // 32) * 32
        return start

    def at(name, shape, dtype, start, offset=0):
        return nc.alloc_sbuf_tensor_at(name, shape, dtype, offset=start + offset)

    KB = 1024
    R_RAW = region(48 * KB)
    R_W = region(32 * KB)
    R_A = region(32 * KB)
    R_B = region(32 * KB)
    R_C = region(41 * KB)
    R_H = region(16 * KB)
    WCH = 2048
    raw = [at(f"raw{s}", [P, WCH], f32, R_RAW, 8 * KB * s) for s in range(6)]
    whi = [at(f"whi{s}", [P, WCH], f32r, R_W, 8 * KB * s) for s in range(2)]
    wlo = [at(f"wlo{s}", [P, WCH], f32r, R_W, 16 * KB + 8 * KB * s) for s in range(2)]
    whi += [at(f"whi{s}", [P, WCH], f32r, R_B, 8 * KB * (s - 2)) for s in (2, 3)]
    wlo += [at(f"wlo{s}", [P, WCH], f32r, R_B, 16 * KB + 8 * KB * (s - 2)) for s in (2, 3)]
    xT_hi = at("xT_hi", [P, KT, SEQ], f32r, R_A)
    xT_lo = at("xT_lo", [P, KT, SEQ], f32r, R_A, 16 * KB)
    mg_hi = at("mg_hi", [P, KT, SEQ], f32r, R_A)
    mg_lo = at("mg_lo", [P, KT, SEQ], f32r, R_A, 16 * KB)
    cT_hi = at("cT_hi", [P, KT, SEQ], f32r, R_A)
    cT_lo = at("cT_lo", [P, KT, SEQ], f32r, R_A, 16 * KB)
    xf = at("xf", [P, TT, D], f32, R_A, 16 * KB)
    gates = at("gates", [P, 2 * KT, SEQ], f32, R_B)
    junk_raw = at("junk_raw", [P, D], f32, R_RAW, 44 * KB)
    junk_a = at("junk_a", [P, D], f32, R_A, 8 * KB)
    hn = at("hn", [P, TT, D], f32, R_B)
    qcT = at("qcT", [P, KT, SEQ], f32, R_B)
    fT = at("fT", [P, KT, SEQ], f32, R_B)
    oT_lo = at("oT_lo", [P, KT, SEQ], f32r, R_B, 16 * KB)
    qaT = at("qaT", [P, H_A, SEQ], f32, R_C)
    kaT = at("kaT", [P, H_A, SEQ], f32, R_C, 8 * KB)
    va = at("va", [P, TT, 512], f32, R_C, 16 * KB)
    qbT = at("qbT", [P, 4, SEQ], f32, R_C, 24 * KB)
    kbT = at("kbT", [P, SEQ], f32, R_C, 32 * KB)
    kiT = at("kiT", [P, SEQ], f32, R_C, 34 * KB)
    qiT = at("qiT", [P, 2, SEQ], f32, R_C, 36 * KB)
    vb = at("vb", [P, TT, DH_B], f32, R_C, 40 * KB)
    yaT_hi = at("yaT_hi", [P, 4, SEQ], f32r, R_C)
    yaT_lo = at("yaT_lo", [P, 4, SEQ], f32r, R_C, 8 * KB)
    ybT_hi = at("ybT_hi", [P, 4, SEQ], f32r, R_C, 16 * KB)
    ybT_lo = at("ybT_lo", [P, 4, SEQ], f32r, R_C, 24 * KB)
    mrow = at("mrow", [P, MT, D], f32, R_C)
    kcT = at("kcT", [P, KT, N_MEM], f32, R_C, 8 * KB)
    mT_hi = at("mT_hi", [P, KT, N_MEM], f32r, R_C, 16 * KB)
    mT_lo = at("mT_lo", [P, KT, N_MEM], f32r, R_C, 24 * KB)
    vc = at("vc", [P, MT, D], f32, R_C, 32 * KB)
    oT_hi = at("oT_hi", [P, KT, SEQ], f32r, R_C, 16 * KB)
    gain_f = at("gain_f", [P, D], f32, R_C)
    gain_o = at("gain_o", [P, D], f32, R_C, 4 * KB)
    RT = 1700
    rt = at("rt", [P, RT], f32, R_C, 8 * KB)
    wr = at("wr", [P, KT, NG + NE], f32, R_C, 8 * KB + 4 * RT + 16)
    tri = at("tri", [P, P], bf16, R_C, 40 * KB)
    ones = at("ones", [P, P], bf16, R_C, 40 * KB + 256)
    M_bf = at("M_bf", [P, TT, NE], bf16, R_C, 40 * KB + 512)
    xrow = at("xrow", [P, TT, D], f32, R_H)
    ya = at("ya", [P, TT, 512], f32, R_H)
    yb = at("yb", [P, TT, 512], f32, R_H, 8 * KB)
    h = at("h", [P, TT, D], f32, R_H)
    blk = at("blk", [BLK, D], f32, R_A)
    Xs = at("Xs", [P, KT, 2, BLK], f32r, R_A, 4 * KB)
    Gs = at("Gs", [P, DE], f32, R_A, 8 * KB)
    Us = at("Us", [P, DE], f32, R_A, 10 * KB)
    sg = at("sg", [P, 4, BLK], f32, R_A, 12 * KB)
    ug = at("ug", [P, 4, BLK], f32, R_A, 13 * KB)
    HT = at("HT", [P, 4, BLK], f32, R_A, 14 * KB)
    Ys = at("Ys", [BLK, D], f32, R_C)
    gath = at("gath", [P, 4, D], f32, R_B)
    sbuf = [[at(f"s{a}{m}", [P, SEQ], f32, R_RAW, (32, 36, 24)[a] * KB + 2 * KB * m) for m in (0, 1)]
            for a in range(3)]
    pT = [[at(f"pT{a}{m}", [P, TT, P], f32, R_RAW, (40, 28)[a] * KB + 2 * KB * m) for m in (0, 1)]
          for a in (0, 1)]
    sq = at("sq", [P, 2048], f32, R_RAW, 32 * KB)
    cp = at("cp", [P, 2, TT, N_MEM], f32, R_RAW, 32 * KB)
    cpT = at("cpT", [P, MT, SEQ], f32, R_RAW, 40 * KB)
    R_S = region(8 * KB - 1200)
    small_at = [0]

    def small(name, shape, dtype=f32):
        n = 4
        for s in shape[1:]:
            n *= s
        t = at(name, shape, dtype, R_S, small_at[0])
        small_at[0] += -(-n // 32) * 32
        assert small_at[0] <= 8 * KB - 1200, small_at
        return t

    work = [None, small("work1", [P, 256]), at("work2", [P, 384], f32, R_RAW, 44 * KB),
            at("work3", [P, 512], f32, R_RAW, 46 * KB)]
    dist = small("dist", [P, SEQ])
    ident = small("ident", [P, P])
    cols = small("cols", [P, 41])
    ii = small("ii", [P, BLK])
    wi = small("wi", [P, TT, H_I])
    zero = small("zero", [P, 256])
    neglam = small("neglam", [P, 4])
    ss = small("ss", [P, 16])
    rs = small("rs", [P, 16])
    nw = small("nw", [P, 16])
    vv = small("vv", [P, 16])
    sqr = small("sqr", [P, 16])
    nmax = small("nmax", [P, 3, 4])
    ssum = small("ssum", [P, 3, 4])
    rsum = small("rsum", [P, 3, 4])
    top8 = small("top8", [P, 8])
    g12 = small("g12", [P, TOPK, TT])
    slot_i = small("slot_i", [P, TOPK, TT], i32)
    over_i = small("over_i", [P, 1 + MAX_OVER], i32)
    crows = at("crows", [41, P], f32, R_RAW, 32 * KB)
    lamr = at("lamr", [P, 4, DH_A], f32, R_RAW, 34 * KB)
    lamp = at("lamp", [P, 2, DH_A], f32, R_RAW, 36 * KB)

    rt_at = [0]

    def rview(*shape):
        n = 1
        for s in shape:
            n *= s
        v = rt[:, rt_at[0]:rt_at[0] + n]
        rt_at[0] += n
        assert rt_at[0] <= RT
        return v if len(shape) == 1 else v.rearrange("p (a b) -> p a b", b=shape[1])

    rview(64)
    r_iota, r_iotam = rview(NE), rview(NE)
    r_log, r_el, r_tmp = rview(TT, NG + NE), rview(TT, NE), rview(TT, NE)
    r_oh = [rview(TT, NE), rview(TT, NE)]
    r_gmax, r_m1, r_m2, r_least, r_gsum, r_e2, r_d2 = (rview(TT) for _ in range(7))
    r_goh, r_gdif, r_gexp = rview(TT, NG), rview(TT, NG), rview(TT, NG)
    r_rank = rview(TT + 1, NE)
    r_over, r_one, r_end, r_base = (rview(NE) for _ in range(4))
    r_cmp = rview(MAX_OVER, NE)
    r_list = rview(1 + MAX_OVER)

    xslots = nc.dram_tensor("xslots", (N_BLOCKS * BLK, D), f32).ap()
    yslots = nc.dram_tensor("yslots", (N_BLOCKS * BLK, D), f32).ap()

    ps = [nc.alloc_psum_tensor(f"ps{b}", [P, 512], f32) for b in range(8)]

    win = w_in[0].rearrange("(k p) n -> p k n", p=P)
    wg = w_gate[0].rearrange("(k p) n -> p k n", p=P)
    wa = w_branch_a[0].rearrange("(k p) n -> p k n", p=P)
    wb = w_branch_b[0].rearrange("(k p) n -> p k n", p=P)
    wo = w_out[0].rearrange("(k p) n -> p k n", p=P)
    wcq = w_cq[0].rearrange("(k p) n -> p k n", p=P)
    wckv = w_ckv[0].rearrange("(k p) n -> p k n", p=P)
    wco = w_co[0].rearrange("(k p) n -> p k n", p=P)

    chunks = []

    def fm_chunk(src, c0):
        chunks.append((256, [(src[:, :, c0:c0 + 256], 0, KT, 0, 256)]))
        return len(chunks) - 1

    def tm_chunks(src, c0):
        for half in (0, 1):
            chunks.append((512, [(src[:, 4 * half:4 * half + 4, c0:c0 + 512], 0, 4, 0, 512)]))
        return len(chunks) - 2

    chunks.append((256, [(win[:, :, c:c + 64], 0, KT, o, 64)
                         for o, c in ((0, C_KB), (64, C_KB), (128, C_KI), (192, C_KI))]))
    CH_K = 0
    CH_QI = fm_chunk(win, C_QI)
    chunks.append((68, [(win[:, :, C_VB:C_VB + 64], 0, KT, 0, 64), (win[:, :, C_WI:C_WI + 4], 0, KT, 64, 4)]))
    CH_VBWI = 2
    CH_QA = [fm_chunk(win, C_QA + 256 * j) for j in (0, 1)]
    CH_KA = [fm_chunk(win, C_KA + 256 * j) for j in (0, 1)]
    CH_VA = tm_chunks(win, C_VA)
    CH_QB = [fm_chunk(win, C_QB + 256 * j) for j in (0, 1)]
    CH_G = [fm_chunk(wg, 256 * j) for j in range(8)]
    CH_BR = []
    for j in range(4):
        chunks.append((256, [(wa[:, :, 256 * j:256 * j + 256], 0, 4, 0, 256),
                             (wb[:, :, 256 * j:256 * j + 256], 4, 8, 0, 256)]))
        CH_BR.append(len(chunks) - 1)
    CH_WO = [tm_chunks(wo, 512 * n) for n in (0, 1)]
    CH_CK = [fm_chunk(wckv, 256 * j) for j in range(4)]
    CH_CV = [tm_chunks(wckv, D + 512 * n) for n in (0, 1)]
    CH_CQ = [fm_chunk(wcq, 256 * j) for j in range(4)]
    CH_CO = [tm_chunks(wco, 512 * n) for n in (0, 1)]
    NCH = len(chunks)
    RING = 3
    raw_dmas = [0] * 6
    raw_need = []
    for n, (_, parts) in enumerate(chunks):
        raw_dmas[n % RING] += len(parts)
        raw_need.append(16 * raw_dmas[n % RING])

    def chunk_cols(n):
        ncol, parts = chunks[n]
        return ncol * max(k1 for _, _, k1, _, _ in parts)

    A_UNITS = [("A", qt, hd) for qt in range(TT) for hd in range(H_A)]
    B_UNITS = [("B", qt, pair) for qt in range(TT) for pair in range(H_B // 2)]
    UNITS = A_UNITS + B_UNITS
    steps = [("cols",), ("norm", "x"), ("split", 0), ("split", 1)]
    steps += [("xT", k) for k in range(KT)]

    def fm(n, js=(0, 1)):
        for j in js:
            steps.append(("fm", n, j))
        if n + 2 < NCH:
            steps.append(("split", n + 2))

    def tm(n, kind):
        steps.append(("tm", n, kind, 0))
        steps.append(("split", n + 2))
        steps.append(("tm", n, kind, 1))
        steps.extend([("tmout", n, kind)])
        if n + 3 < NCH:
            steps.append(("split", n + 3))

    fm(CH_K)
    fm(CH_QI)
    steps.append(("vbwi",))
    steps.append(("split", CH_VBWI + 2))
    rounds = [(qt, r) for qt in range(1, TT) for r in range(NROUND)]
    per = -(-len(rounds) // 8)

    def topk():
        take, rounds[:] = rounds[:per], rounds[per:]
        steps.extend(("topk", qt, r) for qt, r in take)

    for qt in range(1, TT):
        for hd in range(H_I):
            steps.append(("index", qt, hd))
    for n in CH_QA + CH_KA:
        fm(n)
        topk()
    tm(CH_VA, "va")
    topk()
    topk()
    for n in CH_QB:
        fm(n)
        topk()
    gate_tiles = [(CH_G[g // 2], g % 2) for g in range(2 * KT)]
    steps += [("score", 0), ("score", 1), ("score", 2)]
    for u in range(len(UNITS)):
        steps.append(("fin", u))
        steps.append(("tr", u))
        if u + 3 < len(UNITS):
            steps.append(("score", u + 3))
        if u % 2 == 0 and gate_tiles:
            n, j = gate_tiles.pop(0)
            steps.append(("fm", n, j))
            if j == 1:
                steps.append(("split", n + 2))
        steps.append(("av", u))
    steps += [("yanorm",)] + [("yT", "b", j) for j in range(4)] + [("yT", "a", j) for j in range(4)]
    for n in CH_BR:
        for j in (0, 1):
            steps.append(("merge", n, j))
        steps.append(("split", n + 2))
    steps.append(("norm", "mem"))
    tm(CH_WO[0], "wo0")
    steps += [("mT", k) for k in range(KT)]
    tm(CH_WO[1], "wo1")
    steps.append(("norm", "h1"))
    for n in CH_CK:
        fm(n)
    tm(CH_CV[0], "vc0")
    tm(CH_CV[1], "vc1")
    steps += [("cT", k) for k in range(KT)]
    fm(CH_CQ[0])
    steps.append(("cscore", 0))
    fm(CH_CQ[1])
    steps += [("cscore", 1), ("cfin", 0), ("ctr", 0)]
    fm(CH_CQ[2])
    steps += [("cav", 0), ("cscore", 2), ("cfin", 1), ("ctr", 1)]
    fm(CH_CQ[3])
    steps += [("cav", 1), ("cscore", 3), ("cfin", 2), ("ctr", 2)]
    n = CH_CO[0]
    steps += [("cav", 2), ("tm", n, "co0", 0), ("split", n + 2), ("cfin", 3), ("ctr", 3), ("cav", 3),
              ("tm", n, "co0", 1), ("tmout", n, "co0"), ("split", n + 3)]
    tm(CH_CO[1], "co1")
    steps = [s for s in steps if s[0] != "split" or s[1] < NCH]
    steps += [("norm", "h2")] + [("fT", k) for k in range(KT)] + [("logits",), ("rank",)]

    use, fills = {}, [0]

    def fill(*key):
        use[key] = (fills[0] % 8, fills[0] // 8)
        fills[0] += 1

    for s in steps:
        kind = s[0]
        if kind in ("cols", "xT", "mT", "cT", "fT", "fm", "vbwi", "index", "yT", "logits", "rank", "av"):
            fill(*s)
        elif kind == "tm" and s[3] == 0:
            for t in range(MT if s[2][:2] == "vc" else TT):
                fill("tm", s[1], t)
        elif kind in ("score", "tr"):
            u = UNITS[s[1]]
            for m in range(1 if (kind, u[0]) == ("tr", "A") else 2):
                fill(kind, s[1], m)
        elif kind in ("merge", "cscore", "ctr", "cav"):
            for m in (0, 1):
                fill(*s, m)
    bank_uses = [max([n + 1 for b, n in use.values() if b == bank] or [0]) for bank in range(8)]

    sem = nc.alloc_semaphore
    bank_full = [sem(f"bank_full{b}") for b in range(8)]
    bank_free = [sem(f"bank_free{b}") for b in range(8)]
    raw_loaded = [sem(f"raw_loaded{s}") for s in range(6)]
    w_hi, w_lo, half_used = sem("w_hi"), sem("w_lo"), sem("half_used")
    in_loaded, mem_loaded, h_loaded, gain_loaded = (sem(n) for n in ("in_loaded", "mem_loaded", "h_loaded", "gain_loaded"))
    x_loaded = [sem(f"x_loaded{t}") for t in range(TT)]
    const_done, zeroed = sem("const_done"), sem("zeroed")
    lam_sum, lam_exp = sem("lam_sum"), sem("lam_exp")
    n_sum, n_mean, n_root, n_out = (sem(n) for n in ("norm_sum", "norm_mean", "norm_root", "norm_out"))
    act_hi = sem("act_hi")
    index_added = sem("index_added")
    max_done, exp_done, fin_done = sem("max_done"), sem("exp_done"), sem("fin_done")
    sig_done, mg_sum, mg_high, mg_low = sem("sig_done"), sem("mg_sum"), sem("mg_high"), sem("mg_low")
    cmax_done, cfin_done = sem("cmax_done"), sem("cfin_done")
    onehots, route_in, route_exp = sem("onehots"), sem("route_in"), sem("route_exp")
    slots_done = sem("slots_done")
    scattered = sem("scattered")
    dve_chain, act_chain, pool_chain = sem("dve_chain"), sem("act_chain"), sem("pool_chain")
    blk_loaded, xt_done, xs_hi, xs_lo = sem("blk_loaded"), sem("xt_done"), sem("xs_hi"), sem("xs_lo")
    e_whi, e_wlo, e_wused = sem("e_whi"), sem("e_wlo"), sem("e_wused")
    w2_used = sem("w2_used")
    gs_done, us_done, gt_done, ut_done = sem("gs_done"), sem("us_done"), sem("gt_done"), sem("ut_done")
    sg_done, ug_done, ht_done = sem("sg_done"), sem("ug_done"), sem("ht_done")
    ys_act, ys_dve = sem("ys_act"), sem("ys_dve")
    all_stored = sem("all_stored")
    y_stored = sem("y_stored")
    gathered = [sem(f"gathered{b}") for b in range(4)]
    comb_done, out_done = sem("comb_done"), sem("out_done")

    NORMS, SUM_UPTO, OUT_UPTO, NORM_NO = {}, {}, {}, {}
    for name, tiles in (("x", TT), ("ya", 1), ("mem", MT), ("h1", TT), ("h2", TT), ("out", TT)):
        NORM_NO[name] = len(NORMS) + 1
        NORMS[name] = tiles
        SUM_UPTO[name] = sum(NORMS.values())
    T_NO = {}
    for s in steps:
        if s[0] in ("xT", "yT", "mT", "cT"):
            T_NO[s] = len(T_NO) + 1

    def kv(qt):
        return P * (qt + 1)

    halves = [s[1] for s in steps if s[0] == "tm" and s[3] == 0]

    def used_when(n):
        if n in halves:
            return half_used, halves.index(n) + 1
        if n - 1 in halves:
            key = ("tm", n - 1, (MT if n - 1 in CH_CV else TT) - 1)
        elif n == CH_VBWI:
            key = ("vbwi",)
        elif n in CH_BR:
            key = ("merge", n, 1, 1)
        else:
            key = ("fm", n, 1)
        return bank_full[use[key][0]], use[key][1] + 1

    MERGES = [s for s in steps if s[0] == "merge"]
    LAST_CAV = ("cav", H_X - 1, 1)
    E_RAW = [16 * n for n in raw_dmas]

    w1v = w1[0].rearrange("e (k p) n -> e p k n", p=P)
    w3v = w3[0].rearrange("e (k p) n -> e p k n", p=P)
    w2v = w2[0].rearrange("e (k p) n -> e p k n", p=P)

    def expert_src(e, c):
        v = (w1v, w3v, w2v)[c // 2]
        ks = 4 if c < 4 else 2
        if isinstance(e, int):
            return v[e, :, ks * (c % 2):ks * (c % 2) + ks, :]
        return v[bass.ds(e, 1), :, ks * (c % 2):ks * (c % 2) + ks, :].rearrange("e p k n -> (e p) k n")

    def rows_of(slots, i):
        if isinstance(i, int):
            return slots[i * BLK:(i + 1) * BLK, :]
        return slots[bass.ds(i * BLK, BLK), :]

    def raw_view(c):
        return raw[c][:, :].rearrange("p (k n) -> p k n", n=512 if c < 4 else D)

    block = nc.Block()
    with block:

        @block.sync
        def _(sp):
            sp.dma_start(crows[0:8, :], mix_norm[0].rearrange("(k p) -> k p", p=P)).then_inc(in_loaded, 16)
            sp.dma_start(crows[8:16, :], cross_norm[0].rearrange("(k p) -> k p", p=P)).then_inc(in_loaded, 16)
            sp.dma_start(crows[16:24, :], mem_norm[0].rearrange("(k p) -> k p", p=P)).then_inc(in_loaded, 16)
            sp.dma_start(crows[24:40, :], b_gate[0].rearrange("(k p) -> k p", p=P)).then_inc(in_loaded, 16)
            sp.dma_start(crows[40:41, :], diff_subln).then_inc(in_loaded, 16)
            for i, v in enumerate((lam_q1, lam_k1, lam_q2, lam_k2)):
                sp.dma_start(lamr[:, i, :], v[0, :].partition_broadcast(P)).then_inc(in_loaded, 16)

            def load_chunk(n):
                if n >= RING:
                    sp.wait_ge(w_lo, n - RING + 1)
                ncol, parts = chunks[n]
                dst = raw[n % RING][:, 0:chunk_cols(n)].rearrange("p (k n) -> p k n", n=ncol)
                for src, k0, k1, c0, nc_ in parts:
                    sp.dma_start(dst[:, k0:k1, c0:c0 + nc_], src).then_inc(raw_loaded[n % RING], 16)

            for s in steps:
                if s == ("norm", "mem"):
                    sp.wait_ge(mg_low, len(MERGES))
                    sp.dma_start(mrow[:, :, :], mem[0].rearrange("(t p) n -> p t n", p=P)).then_inc(mem_loaded, 16)
                    b, n = use[("yT", "a", 3)]
                    sp.wait_ge(bank_free[b], n + 1)
                    sp.dma_start(h[:, :, :], x[0].rearrange("(t p) n -> p t n", p=P)).then_inc(h_loaded, 16)
                elif s == ("norm", "h2"):
                    b, n = use[LAST_CAV]
                    sp.wait_ge(bank_full[b], n + 1)
                    sp.dma_start(gain_f[:, :], ffn_norm[0, :].partition_broadcast(P)).then_inc(gain_loaded, 16)
                    sp.dma_start(gain_o[:, :], final_norm.partition_broadcast(P)).then_inc(gain_loaded, 16)
                    sp.dma_start(wr[:, :, 0:NG], w_group[0].rearrange("(k p) n -> p k n", p=P)).then_inc(gain_loaded, 16)
                    sp.dma_start(wr[:, :, NG:], w_router[0].rearrange("(k p) n -> p k n", p=P)).then_inc(gain_loaded, 16)
                    sp.dma_start(rt[:, 0:NG], b_group[0, :].partition_broadcast(P)).then_inc(gain_loaded, 16)
                    sp.dma_start(rt[:, NG:NG + NE], b_router[0, :].partition_broadcast(P)).then_inc(gain_loaded, 16)
                    for c in range(4):
                        sp.wait_ge(w_lo, NCH)
                        sp.dma_start(raw_view(c), expert_src(0, c)).then_inc(raw_loaded[c], 16)
                elif s[0] == "split":
                    if s[1] == 0:
                        for n in range(RING - 1):
                            load_chunk(n)
                    if s[1] + RING - 1 < NCH:
                        load_chunk(s[1] + RING - 1)

            with sp.Fori(1, NE) as i:
                for c in range(4):
                    sp.wait_ge(e_wlo, i * 4 - 3 + c)
                    sp.dma_start(raw_view(c), expert_src(i, c)).then_inc(raw_loaded[c], 16)
            sp.wait_ge(slots_done, 1)
            n_over = sp.value_load(over_i[0:1, 0:1], min_val=0, max_val=MAX_OVER)
            with sp.If(n_over > 0):
                with sp.Fori(NE, n_over + NE) as i:
                    e = sp.value_load(over_i[0:1, bass.ds(i - (NE - 1), 1)], min_val=0, max_val=NE - 1)
                    for c in range(4):
                        sp.wait_ge(e_wlo, i * 4 - 3 + c)
                        sp.dma_start(raw_view(c), expert_src(e, c)).then_inc(raw_loaded[c], 16)
            for t in range(TT):
                sp.wait_ge(n_out, SUM_UPTO["h2"] + t + 1)
                sp.dma_start(out[0, P * t:P * t + P, :], h[:, t, :]).then_inc(out_done, 16)
            sp.wait_ge(out_done, 16 * TT)

        @block.gpsimd
        def _(pool):
            links = [0]

            def link(ins):
                links[0] += 1
                ins.then_inc(pool_chain, 1)
                pool.wait_ge(pool_chain, links[0])

            link(pool.memset(ident[:, :], 0.0))
            link(pool.affine_select(out=ident[:, :], in_=ident[:, :], compare_op=ALU.not_equal, fill=1.0,
                                    base=0, pattern=[[-1, P]], channel_multiplier=1))
            link(pool.memset(ii[:, :], 0.0))
            for base in (0, -BLK):
                link(pool.affine_select(out=ii[:, :], in_=ii[:, :], compare_op=ALU.not_equal, fill=1.0,
                                        base=base, pattern=[[-1, BLK]], channel_multiplier=1))
            link(pool.memset(zero[:, :], 0.0))
            pool.iota(dist[:, :], pattern=[[-1, SEQ]], base=SEQ - P, channel_multiplier=1,
                      allow_small_or_imprecise_dtypes=True).then_inc(const_done, 1)
            pool.wait_ge(raw_loaded[CH_QB[0] % RING], raw_need[CH_QB[0]])
            pool.dma_start(xslots.rearrange("(p a) (b n) -> p (a b) n", p=P, n=256),
                           zero[:, :].rearrange("p (o n) -> p o n", o=1).to_broadcast([P, N_BLOCKS * BLK * 4 // P, 256])
                           ).then_inc(zeroed, 16)
            pool.dma_start(yslots[NE * BLK:, :].rearrange("(p a) (b n) -> p (a b) n", p=P, n=256),
                           zero[:, :].rearrange("p (o n) -> p o n", o=1).to_broadcast([P, (N_BLOCKS - NE) * BLK * 4 // P, 256])
                           ).then_inc(zeroed, 16)
            b, n = use[LAST_CAV]
            pool.wait_ge(bank_full[b], n + 1)
            for c in (4, 5):
                pool.dma_start(raw_view(c), expert_src(0, c)).then_inc(raw_loaded[c], 16)
            link(pool.memset(ones[:, :], 1.0))
            link(pool.affine_select(out=tri[:, :], in_=ones[:, :], compare_op=ALU.is_gt, fill=0.0,
                                    base=0, pattern=[[1, P]], channel_multiplier=-1))
            pool.iota(rt[:, 64:64 + NE], pattern=[[1, NE]], base=0, channel_multiplier=0,
                      allow_small_or_imprecise_dtypes=True).then_inc(const_done, 1)
            pool.wait_ge(slots_done, 1)
            pool.wait_ge(zeroed, 32)
            for k in range(TOPK):
                for t in range(TT):
                    pool.indirect_dma_start(
                        out=xslots, out_offset=bass.IndirectOffsetOnAxis(ap=slot_i[:, k, t:t + 1], axis=0),
                        in_=xf[:, t, :], in_offset=None).then_inc(scattered, 16)
            pool.wait_ge(scattered, 16 * TOPK * TT)
            pool.dma_start(blk[:, :], xslots[0:BLK, :]).then_inc(blk_loaded, 16)

            def body(i, e):
                pool.wait_ge(xt_done, i + 1)
                pool.dma_start(blk[:, :], rows_of(xslots, i + 1)).then_inc(blk_loaded, 16)
                if e is not None:
                    for c in (4, 5):
                        pool.wait_ge(w2_used, i * 2 + (c - 4))
                        pool.dma_start(raw_view(c), expert_src(e, c)).then_inc(raw_loaded[c], 16)

            body(0, None)
            with pool.Fori(1, NE) as i:
                body(i, i)
            n_over = pool.value_load(over_i[0:1, 0:1], min_val=0, max_val=MAX_OVER)
            with pool.If(n_over > 0):
                with pool.Fori(NE, n_over + NE) as i:
                    body(i, pool.value_load(over_i[0:1, bass.ds(i - (NE - 1), 1)], min_val=0, max_val=NE - 1))
            pool.wait_ge(y_stored, n_over * 16 + 16 * (NE + 1))
            pool.sem_inc(all_stored, 1)
            pool.wait_ge(all_stored, 1)
            for t in range(TT):
                for k in range(TOPK):
                    b = (2 * t + k) % 4
                    if 2 * t + k >= 4:
                        pool.wait_ge(comb_done, 2 * t + k - 3)
                    pool.indirect_dma_start(
                        out=gath[:, b, :], out_offset=None, in_=yslots,
                        in_offset=bass.IndirectOffsetOnAxis(ap=slot_i[:, k, t:t + 1], axis=0)).then_inc(gathered[b], 16)

        @block.scalar
        def _(act):
            def tile_of(*key):
                b, n = use[key]
                act.wait_ge(bank_full[b], n + 1)
                return ps[b]

            def freed(*key):
                return bank_free[use[key][0]]

            def copied(*key):
                b, n = use[key]
                act.wait_ge(bank_free[b], n + 1)

            def root(name, cols_):
                act.wait_ge(n_mean, NORM_NO[name])
                act.activation(sqr[:, 0:cols_], vv[:, 0:cols_], ACT.Sqrt).then_inc(n_root, 1)

            def norm(name):
                src = {"x": xrow, "mem": mrow}.get(name, h)
                if name == "mem":
                    act.wait_ge(mem_loaded, 16)
                for t in range(NORMS[name]):
                    if SUM_UPTO[name] - NORMS[name] + t:
                        act.wait_ge(n_sum, SUM_UPTO[name] - NORMS[name] + t)
                    if name == "x":
                        act.wait_ge(x_loaded[t], 16)
                    if name in ("h1", "h2"):
                        for n in CH_WO if name == "h1" else CH_CO:
                            copied("tm", n, t)
                    if name == "out":
                        act.wait_ge(comb_done, 2 * (t + 1))
                    act.activation((junk_a if name in ("h2", "out") else junk_raw)[:, :], src[:, t, :], ACT.Square, accum_out=ss[:, t:t + 1]).then_inc(n_sum, 1)
                root(name, NORMS[name])

            for t in range(TT):
                act.dma_start(xrow[:, t, :], x[0, P * t:P * t + P, :]).then_inc(x_loaded[t], 16)
            for s in steps:
                kind = s[0]
                if kind == "cols":
                    p = tile_of(*s)
                    act.activation(cols[:, 0:40], p[:, 0:40], ACT.Copy)
                    act.activation(cols[:, 40:41], p[:, 40:41], ACT.Copy, scale=1.0 - LAMBDA_INIT).then_inc(freed(*s), 1)
                    act.wait_ge(lam_sum, 1)
                    act.activation(neglam[:, 0:2], neglam[:, 2:4], ACT.Exp).then_inc(lam_exp, 1)
                elif kind == "norm":
                    norm(s[1])
                elif kind == "split":
                    n = s[1]
                    act.wait_ge(raw_loaded[n % RING], raw_need[n])
                    if n >= 2:
                        act.wait_ge(*used_when(n - 2))
                    w = chunk_cols(n)
                    act.activation(whi[n % 2][:, 0:w], raw[n % RING][:, 0:w], ACT.Copy).then_inc(w_hi, 1)
                elif kind in ("xT", "mT", "cT"):
                    k = s[1]
                    ncol = N_MEM if kind == "mT" else SEQ
                    dst, g0 = {"xT": (xT_hi, 0), "mT": (mT_hi, 16), "cT": (cT_hi, 8)}[kind]
                    p = tile_of(*s)
                    if s == ("xT", 0):
                        copied("cols")
                    act.activation(dst[:, k, :], p[:, 0:ncol], ACT.Copy,
                                   scale=cols[:, g0 + k:g0 + k + 1]).then_inc(act_hi, 1)
                elif kind == "yT":
                    br, j = s[1:]
                    p = tile_of(*s)
                    if br == "a":
                        act.activation(yaT_hi[:, j, :], p[:, :], ACT.Copy, scale=cols[:, 40:41]).then_inc(act_hi, 1)
                    else:
                        act.activation(ybT_hi[:, j, :], p[:, :], ACT.Copy).then_inc(act_hi, 1)
                elif kind == "fT":
                    act.activation(fT[:, s[1], :], tile_of(*s)[:, :], ACT.Copy).then_inc(freed(*s), 1)
                elif kind == "fm":
                    n, j = s[1:]
                    p = tile_of(*s)
                    if n == CH_K:
                        act.activation((kbT, kiT)[j][:, :], p[:, :], ACT.Copy).then_inc(freed(*s), 1)
                    elif n == CH_QI:
                        act.activation(qiT[:, j, :], p[:, :], ACT.Copy).then_inc(freed(*s), 1)
                    elif n in CH_QA:
                        act.activation(qaT[:, 2 * CH_QA.index(n) + j, :], p[:, :], ACT.Copy,
                                       scale=DH_A ** -0.5).then_inc(freed(*s), 1)
                    elif n in CH_KA:
                        act.activation(kaT[:, 2 * CH_KA.index(n) + j, :], p[:, :], ACT.Copy).then_inc(freed(*s), 1)
                    elif n in CH_QB:
                        act.activation(qbT[:, 2 * CH_QB.index(n) + j, :], p[:, :], ACT.Copy,
                                       scale=DH_B ** -0.5).then_inc(freed(*s), 1)
                    elif n in CH_G:
                        g = 2 * CH_G.index(n) + j
                        act.activation(gates[:, g, :], p[:, :], ACT.Identity,
                                       bias=cols[:, 24 + g:25 + g]).then_inc(freed(*s), 1)
                    elif n in CH_CK:
                        act.activation(kcT[:, 2 * CH_CK.index(n) + j, :], p[:, 0:N_MEM], ACT.Copy).then_inc(freed(*s), 1)
                    elif n in CH_CQ:
                        act.activation(qcT[:, 2 * CH_CQ.index(n) + j, :], p[:, :], ACT.Copy,
                                       scale=DH_X ** -0.5).then_inc(freed(*s), 1)
                elif kind == "vbwi":
                    p = tile_of(*s)[:, 0:TT * 68].rearrange("p (t n) -> p t n", n=68)
                    act.activation(wi[:, :, :], p[:, :, 64:68], ACT.Copy, scale=H_I ** -0.5 * D_I ** -0.5)
                    act.activation(vb[:, :, :], p[:, :, 0:64], ACT.Copy).then_inc(freed(*s), 1)
                elif kind == "tmout" and s[2] in ("va", "vc0", "vc1"):
                    n, what = s[1:]
                    for t in range(MT if what != "va" else TT):
                        p = tile_of("tm", n, t)
                        dst = va[:, t, :] if what == "va" else vc[:, t, 512 * int(what[2]):512 * int(what[2]) + 512]
                        act.activation(dst, p[:, :], ACT.Copy).then_inc(freed("tm", n, t), 1)
                elif kind == "index":
                    qt, hd = s[1:]
                    q = (qt - 1) * H_I + hd
                    p = tile_of(*s)
                    if q >= 2:
                        act.wait_ge(index_added, q - 1)
                    act.activation(sbuf[1][q % 2][:, 0:kv(qt)], p[:, 0:kv(qt)], ACT.Relu).then_inc(freed(*s), 1)
                elif kind == "score":
                    u = s[1]
                    _, qt, _ = UNITS[u]
                    for m in (0, 1):
                        act.wait_ge(max_done, 2 * u + m + 1)
                        b = sbuf[u % 3][m][:, 0:kv(qt)]
                        act.activation(b, b, ACT.Exp, bias=nmax[:, u % 3, m:m + 1],
                                       accum_out=ssum[:, u % 3, m:m + 1]).then_inc(exp_done, 1)
                elif kind == "tr":
                    u = s[1]
                    br, qt, _ = UNITS[u]
                    for m in range(1 if br == "A" else 2):
                        p = tile_of("tr", u, m)
                        if u >= 2:
                            tile_of("av", u - 2)
                        act.activation(pT[u % 2][m][:, 0:qt + 1, :], p[:, 0:kv(qt)].rearrange("p (s q) -> p s q", q=P),
                                       ACT.Copy).then_inc(freed("tr", u, m), 1)
                elif kind == "av":
                    u = s[1]
                    br, qt, j = UNITS[u]
                    if br == "A":
                        act.activation(ya[:, qt, P * j:P * j + P], tile_of(*s)[:, 0:P], ACT.Copy,
                                       scale=rsum[:, u % 3, 0:1]).then_inc(freed(*s), 1)
                elif kind == "yanorm":
                    copied("av", len(A_UNITS) - 1)
                    tile_of("av", len(UNITS) - 1)
                    act.activation(sq[:, :], ya[:, :, :].rearrange("p t n -> p (t n)"), ACT.Square).then_inc(n_sum, 1)
                    root("ya", 16)
                    for g in range(0, 2 * KT, 4):
                        v = gates[:, g:g + 4, :].rearrange("p g n -> p (g n)")
                        act.activation(v, v, ACT.Sigmoid).then_inc(sig_done, 1)
                elif kind == "merge":
                    i = MERGES.index(s)
                    act.wait_ge(mg_sum, i + 1)
                    act.activation(mg_hi[:, i, :], gates[:, i, :], ACT.Copy).then_inc(mg_high, 1)
                elif kind == "cscore":
                    hx = s[1]
                    for m in (0, 1):
                        act.wait_ge(cmax_done, 2 * hx + m + 1)
                        for a in (0, 1):
                            qt = 2 * m + a
                            e = act.activation(cp[:, hx % 2, qt, :],
                                               ps[use[("cscore", hx, m)][0]][:, N_MEM * a:N_MEM * a + N_MEM],
                                               ACT.Exp, bias=nmax[:, hx % 2, qt:qt + 1],
                                               accum_out=ssum[:, hx % 2, qt:qt + 1])
                        e.then_inc(freed("cscore", hx, m), 1)
                elif kind == "ctr":
                    hx = s[1]
                    for m in range(MT):
                        p = tile_of("ctr", hx, m)
                        if hx >= 1:
                            tile_of("cav", hx - 1, 1)
                        act.activation(cpT[:, m, :], p[:, :], ACT.Copy).then_inc(freed("ctr", hx, m), 1)
                elif kind == "cav":
                    hx = s[1]
                    for m in (0, 1):
                        act.activation(oT_hi[:, 2 * hx + m, :], tile_of("cav", hx, m)[:, :], ACT.Copy).then_inc(act_hi, 1)
            act.wait_ge(route_in, 1)
            act.activation(r_gexp, r_gdif, ACT.Exp).then_inc(route_exp, 1)
            act.wait_ge(route_in, 2)
            act.activation(r_e2, r_d2, ACT.Exp).then_inc(route_exp, 1)

            def split_hi(i, c):
                act.wait_ge(raw_loaded[c], i * 16 + (E_RAW[c] + 16))
                act.wait_ge(e_wused, i * 4 + (c - 2))
                act.activation(whi[c][:, :], raw[c][:, :], ACT.Copy).then_inc(e_whi, 1)

            def rows_hi(i):
                act.wait_ge(xt_done, i + 1)
                act.wait_ge(e_wused, i * 4 + 1)
                act.activation(Xs[:, :, 0, :], ps[0][:, :].rearrange("p (k n) -> p k n", n=BLK),
                               ACT.Copy).then_inc(xs_hi, 1)

            def output(i):
                act.wait_ge(w2_used, i * 2 + 3)
                act.wait_ge(y_stored, i * 16 + 16)
                act.activation(Ys[:, 0:512], ps[4][0:BLK, :], ACT.Copy).then_inc(ys_act, 1)
                act.wait_ge(ys_act, i + 2)
                act.wait_ge(ys_dve, i + 2)
                act.dma_start(rows_of(yslots, i), Ys[:, :]).then_inc(y_stored, 16)

            def body(i, ahead, first=False):
                if ahead:
                    split_hi(i + 1, 0)
                act.wait_ge(e_wused, i * 4 + 3)
                act.wait_ge(gt_done, i + 1)
                act.activation(Gs[:, :], ps[1][:, :], ACT.Copy).then_inc(gs_done, 1)
                if ahead:
                    split_hi(i + 1, 1)
                act.wait_ge(gt_done, i + 2)
                act.wait_ge(ht_done, i + 1)
                act.activation(sg[:, :, :], ps[3][:, 0:4 * BLK].rearrange("p (f n) -> p f n", n=BLK),
                               ACT.Sigmoid).then_inc(sg_done, 1)
                if ahead:
                    split_hi(i + 1, 2)
                act.wait_ge(e_wused, i * 4 + 5)
                act.wait_ge(ut_done, i + 1)
                act.activation(Us[:, :], ps[2][:, :], ACT.Copy).then_inc(us_done, 1)
                rows_hi(i + 1)
                if ahead:
                    split_hi(i + 1, 3)
                if not first:
                    output(i - 1)

            act.sem_inc(gs_done, 1)
            act.sem_inc(us_done, 1)
            act.sem_inc(ys_act, 1)
            act.sem_inc(y_stored, 16)
            b, n = use[("logits",)]
            act.wait_ge(bank_full[b], n + 1)
            for c in range(4):
                act.wait_ge(raw_loaded[c], E_RAW[c] + 16)
                act.activation(whi[c][:, :], raw[c][:, :], ACT.Copy).then_inc(e_whi, 1)
            rows_hi(0)
            body(0, True, first=True)
            with act.Fori(1, NE - 1) as i:
                body(i, True)
            body(NE - 1, False)
            n_over = act.value_load(over_i[0:1, 0:1], min_val=0, max_val=MAX_OVER)
            with act.If(n_over > 0):
                with act.Fori(NE, n_over + NE) as i:
                    for c in range(4):
                        split_hi(i, c)
                    body(i, False)
            output(n_over + (NE - 1))
            norm("out")

        @block.vector
        def _(dve):
            links = [0]

            def link(ins):
                links[0] += 1
                ins.then_inc(dve_chain, 1)
                dve.wait_ge(dve_chain, links[0])

            def tile_of(*key):
                b, n = use[key]
                dve.wait_ge(bank_full[b], n + 1)
                return ps[b]

            def freed(*key):
                return bank_free[use[key][0]]

            def copied(*key):
                b, n = use[key]
                dve.wait_ge(bank_free[b], n + 1)

            def inverse_root(name, n, cols_):
                v, r, w = vv[:, 0:cols_], rs[:, 0:cols_], nw[:, 0:cols_]
                if name != "x":
                    dve.wait_ge(n_out, SUM_UPTO[name] - NORMS[name])
                dve.tensor_scalar(v, ss[:, 0:cols_], 1.0 / n, EPS, ALU.mult, ALU.add).then_inc(n_mean, 1)
                dve.wait_ge(n_root, NORM_NO[name])
                link(dve.reciprocal(r, sqr[:, 0:cols_]))
                link(dve.tensor_tensor(w, r, r, ALU.mult))
                link(dve.tensor_tensor(w, w, v, ALU.mult))
                link(dve.tensor_scalar(w, w, -0.5, 1.5, ALU.mult, ALU.add))
                link(dve.tensor_tensor(r, r, w, ALU.mult))

            def norm(name):
                dve.wait_ge(n_sum, SUM_UPTO[name])
                inverse_root(name, D, NORMS[name])
                if name == "h2":
                    dve.wait_ge(gain_loaded, 16 * 6)
                for t in range(NORMS[name]):
                    r = rs[:, t:t + 1]
                    if name == "x":
                        ins = dve.tensor_scalar(xrow[:, t, :], xrow[:, t, :], r, None, ALU.mult)
                    elif name == "mem":
                        ins = dve.tensor_scalar(mrow[:, t, :], mrow[:, t, :], r, None, ALU.mult)
                    elif name == "h1":
                        ins = dve.tensor_scalar(hn[:, t, :], h[:, t, :], r, None, ALU.mult)
                    elif name == "h2":
                        ins = dve.scalar_tensor_tensor(xf[:, t, :], h[:, t, :], r, gain_f[:, :], ALU.mult, ALU.mult)
                    else:
                        ins = dve.scalar_tensor_tensor(h[:, t, :], h[:, t, :], r, gain_o[:, :], ALU.mult, ALU.mult)
                    ins.then_inc(n_out, 1)

            dve.wait_ge(in_loaded, 16 * 9)
            link(dve.tensor_tensor(lamp[:, :, :], lamr[:, 0:4:2, :], lamr[:, 1:4:2, :], ALU.mult))
            dve.tensor_reduce(neglam[:, 2:4], lamp[:, :, :], AX.X, ALU.add).then_inc(lam_sum, 1)
            dve.wait_ge(const_done, 1)
            link(dve.scalar_tensor_tensor(dist[:, :], dist[:, :], -1.0, dist[:, :], ALU.mult, ALU.max))
            link(dve.memset(dist[0:CHUNK, SEQ - CHUNK:SEQ], BIG))
            dve.wait_ge(lam_exp, 1)
            link(dve.tensor_tensor(neglam[:, 2:3], neglam[:, 1:2], neglam[:, 0:1], ALU.subtract))
            link(dve.tensor_scalar(neglam[:, 0:1], neglam[:, 2:3], -LAMBDA_INIT, None, ALU.add))

            for s in steps:
                kind = s[0]
                if kind == "norm":
                    norm(s[1])
                elif kind == "split":
                    n = s[1]
                    w = chunk_cols(n)
                    dve.wait_ge(w_hi, n + 1)
                    dve.tensor_tensor(wlo[n % 2][:, 0:w], raw[n % RING][:, 0:w],
                                      whi[n % 2][:, 0:w].bitcast(f32), ALU.subtract).then_inc(w_lo, 1)
                elif kind in ("xT", "mT", "cT"):
                    k = s[1]
                    ncol = N_MEM if kind == "mT" else SEQ
                    lo, hi, g0 = {"xT": (xT_lo, xT_hi, 0), "mT": (mT_lo, mT_hi, 16), "cT": (cT_lo, cT_hi, 8)}[kind]
                    dve.wait_ge(act_hi, T_NO[s])
                    dve.scalar_tensor_tensor(lo[:, k, :], tile_of(*s)[:, 0:ncol], cols[:, g0 + k:g0 + k + 1],
                                             hi[:, k, :].bitcast(f32), ALU.mult, ALU.subtract).then_inc(freed(*s), 1)
                elif kind == "yT":
                    br, j = s[1:]
                    dve.wait_ge(act_hi, T_NO[s])
                    if br == "a":
                        dve.scalar_tensor_tensor(yaT_lo[:, j, :], tile_of(*s)[:, :], cols[:, 40:41],
                                                 yaT_hi[:, j, :].bitcast(f32), ALU.mult, ALU.subtract).then_inc(freed(*s), 1)
                    else:
                        dve.tensor_tensor(ybT_lo[:, j, :], tile_of(*s)[:, :], ybT_hi[:, j, :].bitcast(f32),
                                          ALU.subtract).then_inc(freed(*s), 1)
                elif kind == "index":
                    qt, hd = s[1:]
                    q = (qt - 1) * H_I + hd
                    copied(*s)
                    r, w = sbuf[1][q % 2][:, 0:kv(qt)], work[qt][:, :]
                    if hd == 0:
                        dve.tensor_scalar(w, r, wi[:, qt, hd:hd + 1], None, ALU.mult).then_inc(index_added, 1)
                    else:
                        dve.scalar_tensor_tensor(w, r, wi[:, qt, hd:hd + 1], w, ALU.mult, ALU.add).then_inc(index_added, 1)
                    dve.wait_ge(index_added, q + 1)
                    if hd == H_I - 1:
                        link(dve.memset(work[qt][0:CHUNK, kv(qt) - CHUNK:kv(qt)], -BIG))
                elif kind == "topk":
                    qt, r = s[1:]
                    w = work[qt][:, :]
                    link(dve.max(top8[:, :], w))
                    link(dve.match_replace(w, top8[:, :], w, TAKEN))
                    if r == NROUND - 1:
                        link(dve.tensor_scalar(w, w, TAKEN / 3, BIG, ALU.is_gt, ALU.mult))
                        link(dve.tensor_tensor(w, w, dist[:, SEQ - kv(qt):SEQ], ALU.add))
                elif kind == "score":
                    u = s[1]
                    br, qt, j = UNITS[u]
                    for m in (0, 1):
                        if br == "A" or qt == 0:
                            d = dist[:, SEQ - kv(qt):SEQ]
                        else:
                            d = work[qt][:, :]
                        slope = 2.0 ** (-8.0 * (j + 1) / H_A) if br == "A" else 2.0 ** (-8.0 * (2 * j + m + 1) / H_B)
                        p = tile_of("score", u, m)
                        b = sbuf[u % 3][m][:, 0:kv(qt)]
                        if u >= 3 and m == 0:
                            tile_of("tr", u - 3, 0 if UNITS[u - 3][0] == "A" else 1)
                        dve.scalar_tensor_tensor(b, d, -slope, p[:, 0:kv(qt)], ALU.mult, ALU.add).then_inc(freed("score", u, m), 1)
                        copied("score", u, m)
                        dve.tensor_reduce(nmax[:, u % 3, m:m + 1], b, AX.X, ALU.max, negate=True).then_inc(max_done, 1)
                elif kind == "fin":
                    u = s[1]
                    br, qt, _ = UNITS[u]
                    dve.wait_ge(exp_done, 2 * u + 2)
                    if u >= 3:
                        copied("av", u - 3)
                    if br == "A":
                        link(dve.reciprocal(rsum[:, u % 3, 0:2], ssum[:, u % 3, 0:2]))
                        link(dve.tensor_scalar(rsum[:, u % 3, 2:3], rsum[:, u % 3, 1:2], neglam[:, 0:1],
                                               ssum[:, u % 3, 0:1], ALU.mult, ALU.mult))
                        p0, p1 = (sbuf[u % 3][m][:, 0:kv(qt)] for m in (0, 1))
                        dve.scalar_tensor_tensor(p0, p1, rsum[:, u % 3, 2:3], p0, ALU.mult, ALU.add).then_inc(fin_done, 1)
                    else:
                        dve.reciprocal(rsum[:, u % 3, 0:2], ssum[:, u % 3, 0:2]).then_inc(fin_done, 1)
                        dve.wait_ge(fin_done, u + 1)
                elif kind == "av":
                    u = s[1]
                    br, qt, j = UNITS[u]
                    if br == "B":
                        p = tile_of(*s)[:, 0:2 * DH_B].rearrange("p (m n) -> p m n", m=2)
                        dve.tensor_tensor(yb[:, qt, P * j:P * j + P].rearrange("p (m n) -> p m n", m=2), p,
                                          rsum[:, u % 3, 0:2].unsqueeze(2).to_broadcast([P, 2, DH_B]),
                                          ALU.mult).then_inc(freed(*s), 1)
                elif kind == "yanorm":
                    dve.wait_ge(n_sum, SUM_UPTO["ya"])
                    link(dve.tensor_reduce(ss[:, 0:16], sq[:, :].rearrange("p (g n) -> p g n", n=P), AX.X, ALU.add))
                    inverse_root("ya", 2 * DH_A, 16)
                    y = ya[:, :, :].rearrange("p t (j n) -> p (t j) n", n=P)
                    dve.tensor_tensor(y, y, rs[:, 0:16].unsqueeze(2).to_broadcast([P, 16, P]), ALU.mult).then_inc(n_out, 1)
                elif kind == "merge":
                    i = MERGES.index(s)
                    if i == 0:
                        dve.wait_ge(sig_done, 4)
                    g0, g1 = gates[:, i, :], gates[:, KT + i, :]
                    dve.tensor_tensor(g0, tile_of(*s, 0)[:, :], g0, ALU.mult).then_inc(freed(*s, 0), 1)
                    dve.tensor_tensor(g1, tile_of(*s, 1)[:, :], g1, ALU.mult).then_inc(freed(*s, 1), 1)
                    copied(*s, 0)
                    copied(*s, 1)
                    dve.tensor_tensor(g0, g0, g1, ALU.add).then_inc(mg_sum, 1)
                    dve.wait_ge(mg_high, i + 1)
                    dve.tensor_tensor(mg_lo[:, i, :], g0, mg_hi[:, i, :].bitcast(f32), ALU.subtract).then_inc(mg_low, 1)
                elif kind == "tmout" and s[2][:2] in ("wo", "co"):
                    n, what = s[1:]
                    half = int(what[2])
                    if what == "wo0":
                        dve.wait_ge(h_loaded, 16)
                    for t in range(TT):
                        v = h[:, t, 512 * half:512 * half + 512]
                        dve.tensor_tensor(v, tile_of("tm", n, t)[:, :], v, ALU.add).then_inc(freed("tm", n, t), 1)
                elif kind == "cscore":
                    hx = s[1]
                    for m in (0, 1):
                        p = tile_of("cscore", hx, m)[:, :].rearrange("p (a n) -> p a n", a=2)
                        dve.tensor_reduce(nmax[:, hx % 2, 2 * m:2 * m + 2], p, AX.X, ALU.max, negate=True).then_inc(cmax_done, 1)
                elif kind == "cfin":
                    hx = s[1]
                    copied("cscore", hx, 0)
                    copied("cscore", hx, 1)
                    link(dve.reciprocal(rsum[:, hx % 2, 0:TT], ssum[:, hx % 2, 0:TT]))
                    dve.tensor_tensor(cp[:, hx % 2, :, :], cp[:, hx % 2, :, :],
                                      rsum[:, hx % 2, 0:TT].unsqueeze(2).to_broadcast([P, TT, N_MEM]),
                                      ALU.mult).then_inc(cfin_done, 1)
                elif kind == "cav":
                    hx = s[1]
                    for m in (0, 1):
                        dve.wait_ge(act_hi, len(T_NO) + 2 * hx + m + 1)
                        dve.tensor_tensor(oT_lo[:, 2 * hx + m, :], tile_of("cav", hx, m)[:, :],
                                          oT_hi[:, 2 * hx + m, :].bitcast(f32), ALU.subtract).then_inc(freed("cav", hx, m), 1)

            dve.wait_ge(const_done, 2)
            dve.wait_ge(gain_loaded, 16 * 6)
            link(dve.tensor_scalar(r_iotam, r_iota, -99.0, None, ALU.add))
            p = tile_of("logits")[:, 0:TT * (NG + NE)].rearrange("p (t n) -> p t n", t=TT)
            dve.tensor_tensor(r_log, p, rt[:, 0:NG + NE].unsqueeze(1).to_broadcast([P, TT, NG + NE]),
                              ALU.add).then_inc(freed("logits"), 1)
            copied("logits")

            def first_max(values, width, best, onehot, tmp, least):
                wide = [P, TT, width]
                im = r_iotam[:, 0:width].unsqueeze(1).to_broadcast(wide)
                link(dve.tensor_reduce(best, values, AX.X, ALU.max))
                link(dve.tensor_tensor(tmp, values, best.unsqueeze(2).to_broadcast(wide), ALU.is_equal))
                link(dve.tensor_tensor(tmp, tmp, im, ALU.mult))
                link(dve.tensor_reduce(least, tmp, AX.X, ALU.min))
                link(dve.tensor_tensor(onehot, im, least.unsqueeze(2).to_broadcast(wide), ALU.is_equal))

            gl = r_log[:, :, 0:NG]
            first_max(gl, NG, r_gmax, r_goh, r_tmp[:, :, 0:NG], r_least)
            dve.tensor_tensor(r_gdif, gl, r_gmax.unsqueeze(2).to_broadcast([P, TT, NG]), ALU.subtract).then_inc(route_in, 1)
            link(dve.tensor_scalar(r_goh, r_goh, BIG, -BIG, ALU.mult, ALU.add))
            link(dve.tensor_tensor(r_el.rearrange("p t (g e) -> p t g e", g=NG),
                                   r_log[:, :, NG:].rearrange("p t (g e) -> p t g e", g=NG),
                                   r_goh.unsqueeze(3).to_broadcast([P, TT, NG, EPG]), ALU.add))
            first_max(r_el, NE, r_m1, r_oh[0], r_tmp, r_least)
            link(dve.scalar_tensor_tensor(r_el, r_oh[0], -4 * BIG, r_el, ALU.mult, ALU.add))
            first_max(r_el, NE, r_m2, r_oh[1], r_tmp, r_least)
            dve.tensor_tensor(r_d2, r_m2, r_m1, ALU.subtract).then_inc(route_in, 1)
            dve.tensor_tensor(M_bf[:, :, :], r_oh[0], r_oh[1], ALU.add).then_inc(onehots, 1)
            dve.wait_ge(route_exp, 2)
            link(dve.tensor_reduce(r_gsum, r_gexp, AX.X, ALU.add))
            link(dve.scalar_tensor_tensor(r_gsum, r_e2, 1.0, r_gsum, ALU.add, ALU.mult))
            link(dve.reciprocal(g12[:, 0, :], r_gsum))
            link(dve.tensor_tensor(g12[:, 1, :], g12[:, 0, :], r_e2, ALU.mult))
            p = tile_of("rank")[:, 0:(TT + 1) * NE].rearrange("p (t e) -> p t e", e=NE)
            dve.tensor_copy(r_rank, p).then_inc(freed("rank"), 1)
            copied("rank")
            counts = r_rank[:, TT, :]
            link(dve.memset(r_over, 0.0))
            for k in range(1, SEQ // BLK):
                link(dve.scalar_tensor_tensor(r_over, counts, float(BLK * k), r_over, ALU.is_gt, ALU.add))
            link(dve.memset(r_one, 1.0))
            link(dve.tensor_tensor_scan(r_end, r_one, r_over, 0.0, ALU.mult, ALU.add))
            link(dve.tensor_tensor(r_base, r_end, r_over, ALU.subtract))
            link(dve.tensor_tensor(r_base, r_base, r_iota, ALU.subtract))
            link(dve.tensor_scalar(r_base, r_base, float(BLK), float(BLK * NE - BLK), ALU.mult, ALU.add))
            rank = r_rank[:, 0:TT, :]
            link(dve.tensor_scalar(r_tmp, rank, float(BLK), None, ALU.is_ge))
            link(dve.tensor_tensor(r_tmp, r_tmp, r_base.unsqueeze(1).to_broadcast([P, TT, NE]), ALU.mult))
            link(dve.tensor_tensor(r_tmp, r_tmp, rank, ALU.add))
            link(dve.tensor_scalar(r_one, r_iota, float(BLK), None, ALU.mult))
            link(dve.tensor_tensor(r_tmp, r_tmp, r_one.unsqueeze(1).to_broadcast([P, TT, NE]), ALU.add))
            for k in range(TOPK):
                link(dve.tensor_tensor(r_oh[k], r_oh[k], r_tmp, ALU.mult))
                link(dve.tensor_reduce(r_least, r_oh[k], AX.X, ALU.add))
                link(dve.tensor_copy(slot_i[:, k, :], r_least))
            wide = [P, MAX_OVER, NE]
            link(dve.tensor_tensor(r_cmp, r_end.unsqueeze(1).to_broadcast(wide),
                                   r_iota[:, 0:MAX_OVER].unsqueeze(2).to_broadcast(wide), ALU.is_le))
            link(dve.tensor_reduce(r_list[:, 1:], r_cmp, AX.X, ALU.add))
            link(dve.tensor_scalar(r_list[:, 1:], r_list[:, 1:], float(NE - 1), None, ALU.min))
            link(dve.tensor_copy(r_list[:, 0:1], r_end[:, NE - 1:NE]))
            dve.tensor_copy(over_i[:, :], r_list).then_inc(slots_done, 1)

            def split_lo(i, c):
                dve.wait_ge(e_whi, i * 4 + (c + 1))
                dve.tensor_tensor(wlo[c][:, :], raw[c][:, :], whi[c][:, :].bitcast(f32), ALU.subtract).then_inc(e_wlo, 1)

            def rows_lo(i):
                dve.wait_ge(xs_hi, i + 1)
                dve.tensor_tensor(Xs[:, :, 1, :], ps[0][:, :].rearrange("p (k n) -> p k n", n=BLK),
                                  Xs[:, :, 0, :].bitcast(f32), ALU.subtract).then_inc(xs_lo, 1)

            def output(i):
                dve.wait_ge(w2_used, i * 2 + 3)
                dve.wait_ge(y_stored, i * 16 + 16)
                dve.tensor_copy(Ys[:, 512:1024], ps[5][0:BLK, :]).then_inc(ys_dve, 1)

            def body(i, ahead, first=False):
                if ahead:
                    for c in range(3):
                        split_lo(i + 1, c)
                rows_lo(i + 1)
                if ahead:
                    split_lo(i + 1, 3)
                dve.wait_ge(sg_done, i + 1)
                dve.wait_ge(ut_done, i + 2)
                dve.tensor_tensor(ug[:, :, :], ps[3][:, 4 * BLK:8 * BLK].rearrange("p (f n) -> p f n", n=BLK),
                                  sg[:, :, :], ALU.mult).then_inc(ug_done, 1)
                dve.wait_ge(ug_done, i + 1)
                dve.wait_ge(w2_used, i * 2 + 1)
                dve.tensor_tensor(HT[:, :, :], ps[3][:, 0:4 * BLK].rearrange("p (f n) -> p f n", n=BLK),
                                  ug[:, :, :], ALU.mult).then_inc(ht_done, 1)
                if not first:
                    output(i - 1)

            dve.sem_inc(ht_done, 1)
            dve.sem_inc(ys_dve, 1)
            for c in range(4):
                split_lo(0, c)
            rows_lo(0)
            body(0, True, first=True)
            with dve.Fori(1, NE - 1) as i:
                body(i, True)
            body(NE - 1, False)
            n_over = dve.value_load(over_i[0:1, 0:1], min_val=0, max_val=MAX_OVER)
            with dve.If(n_over > 0):
                with dve.Fori(NE, n_over + NE) as i:
                    for c in range(4):
                        split_lo(i, c)
                    body(i, False)
            output(n_over + (NE - 1))
            for t in range(TT):
                for k in range(TOPK):
                    j = TOPK * t + k
                    dve.wait_ge(gathered[j % 4], 16 * (j // 4 + 1))
                    dve.scalar_tensor_tensor(h[:, t, :], gath[:, j % 4, :], g12[:, k, t:t + 1], h[:, t, :],
                                             ALU.mult, ALU.add).then_inc(comb_done, 1)
                    dve.wait_ge(comb_done, j + 1)
            norm("out")

        @block.tensor
        def _(pe):
            def opened(*key):
                b, n = use[key]
                if n:
                    pe.wait_ge(bank_free[b], n)
                return ps[b]

            def full(*key):
                return bank_full[use[key][0]]

            def copied(*key):
                b, n = use[key]
                pe.wait_ge(bank_free[b], n + 1)

            def product(o, ahi, alo, bhi, blo, start, stop):
                pe.matmul(o, ahi, bhi, start=start, stop=False)
                pe.matmul(o, ahi, blo, start=False, stop=False)
                return pe.matmul(o, alo, bhi, start=False, stop=stop)

            def wview(n):
                ncol = chunks[n][0]
                return (w[n % 2][:, 0:chunk_cols(n)].rearrange("p (k n) -> p k n", n=ncol) for w in (whi, wlo))

            for s in steps:
                kind = s[0]
                if kind == "cols":
                    pe.wait_ge(in_loaded, 16 * 9)
                    pe.wait_ge(const_done, 1)
                    pe.transpose(opened(*s)[:, 0:41], crows[:, :], ident[0:41, 0:41]).then_inc(full(*s), 1)
                elif kind in ("xT", "mT", "cT", "fT"):
                    name, src = {"xT": ("x", xrow), "mT": ("mem", mrow), "cT": ("h1", hn), "fT": ("h2", xf)}[kind]
                    k = s[1]
                    if k == 0:
                        pe.wait_ge(n_out, SUM_UPTO[name])
                    o = opened(*s)
                    for t in range(NORMS[name]):
                        ins = pe.transpose(o[:, P * t:P * t + P], src[:, t, P * k:P * k + P], ident[:, :])
                    ins.then_inc(full(*s), 1)
                elif kind == "yT":
                    br, j = s[1:]
                    if s == ("yT", "b", 0):
                        copied("av", len(UNITS) - 1)
                    if s == ("yT", "a", 0):
                        pe.wait_ge(n_out, SUM_UPTO["ya"])
                    o = opened(*s)
                    for t in range(TT):
                        ins = pe.transpose(o[:, P * t:P * t + P], (ya if br == "a" else yb)[:, t, P * j:P * j + P], ident[:, :])
                    ins.then_inc(full(*s), 1)
                elif kind == "fm":
                    n, j = s[1:]
                    if n in CH_CK:
                        bhi, blo, ncol, src = mT_hi, mT_lo, N_MEM, "mT"
                    elif n in CH_CQ:
                        bhi, blo, ncol, src = cT_hi, cT_lo, SEQ, "cT"
                    else:
                        bhi, blo, ncol, src = xT_hi, xT_lo, SEQ, "xT"
                    if j == 0:
                        pe.wait_ge(w_lo, n + 1)
                    o = opened(*s)[:, 0:ncol]
                    ahi, alo = wview(n)
                    c = slice(P * j, P * j + P)
                    for k in range(KT):
                        if j == 0 and n in (CH_K, CH_CK[0], CH_CQ[0]):
                            copied(src, k)
                        ins = product(o, ahi[:, k, c], alo[:, k, c], bhi[:, k, :], blo[:, k, :], k == 0, k == KT - 1)
                    ins.then_inc(full(*s), 1)
                elif kind == "vbwi":
                    pe.wait_ge(w_lo, CH_VBWI + 1)
                    o = opened(*s)
                    bhi, blo = wview(CH_VBWI)
                    for t in range(TT):
                        a = slice(P * t, P * t + P)
                        for k in range(KT):
                            ins = product(o[:, 68 * t:68 * t + 68], xT_hi[:, k, a], xT_lo[:, k, a],
                                          bhi[:, k, :], blo[:, k, :], k == 0, k == KT - 1)
                    ins.then_inc(full(*s), 1)
                elif kind == "tm":
                    _, n, what, half = s
                    pe.wait_ge(w_lo, n + half + 1)
                    ahi, alo = {"va": (xT_hi, xT_lo), "wo": (mg_hi, mg_lo), "vc": (mT_hi, mT_lo),
                                "co": (oT_hi, oT_lo)}[what[:2]]
                    if half == 0 and what == "wo0":
                        pe.wait_ge(mg_low, KT)
                    if what == "co0":
                        for hx in (2 * half, 2 * half + 1):
                            for m in (0, 1):
                                copied("cav", hx, m)
                    bhi, blo = wview(n + half)
                    for t in range(MT if what[:2] == "vc" else TT):
                        o = opened("tm", n, t) if half == 0 else ps[use[("tm", n, t)][0]]
                        a = slice(P * t, P * t + P)
                        for k in range(4):
                            kk = 4 * half + k
                            ins = product(o[:, :], ahi[:, kk, a], alo[:, kk, a], bhi[:, k, :], blo[:, k, :],
                                          kk == 0, kk == KT - 1)
                        if half == 1:
                            ins.then_inc(full("tm", n, t), 1)
                    if half == 0:
                        ins.then_inc(half_used, 1)
                elif kind == "index":
                    qt, hd = s[1:]
                    if (qt, hd) == (1, 0):
                        for j in (0, 1):
                            copied("fm", CH_K, j)
                            copied("fm", CH_QI, j)
                        copied("vbwi")
                    a = slice(64 * (hd % 2), 64 * (hd % 2) + 64)
                    pe.matmul(opened(*s)[:, 0:kv(qt)], qiT[a, hd // 2, P * qt:P * qt + P], kiT[a, 0:kv(qt)],
                              start=True, stop=True).then_inc(full(*s), 1)
                elif kind == "score":
                    u = s[1]
                    br, qt, j = UNITS[u]
                    if u == 0:
                        for n in CH_QA + CH_KA + CH_QB:
                            for jj in (0, 1):
                                copied("fm", n, jj)
                        for t in range(TT):
                            copied("tm", CH_VA, t)
                    for m in (0, 1):
                        a = slice(64 * m, 64 * m + 64)
                        q = (qaT if br == "A" else qbT)[a, j, P * qt:P * qt + P]
                        k = kaT[a, j, 0:kv(qt)] if br == "A" else kbT[a, 0:kv(qt)]
                        pe.matmul(opened("score", u, m)[:, 0:kv(qt)], q, k, start=True, stop=True).then_inc(full("score", u, m), 1)
                elif kind == "tr":
                    u = s[1]
                    br, qt, _ = UNITS[u]
                    pe.wait_ge(fin_done, u + 1)
                    for m in range(1 if br == "A" else 2):
                        o = opened("tr", u, m)
                        for k in range(qt + 1):
                            ins = pe.transpose(o[:, P * k:P * k + P], sbuf[u % 3][m][:, P * k:P * k + P], ident[:, :])
                        ins.then_inc(full("tr", u, m), 1)
                elif kind == "av":
                    u = s[1]
                    br, qt, j = UNITS[u]
                    o = opened(*s)
                    for m in range(1 if br == "A" else 2):
                        copied("tr", u, m)
                        for k in range(qt + 1):
                            v = va[:, k, P * j:P * j + P] if br == "A" else vb[:, k, :]
                            ins = pe.matmul(o[:, DH_B * m:DH_B * m + (P if br == "A" else DH_B)], pT[u % 2][m][:, k, :], v,
                                            start=(k == 0), stop=(k == qt))
                    ins.then_inc(full(*s), 1)
                elif kind == "merge":
                    _, n, j = s
                    if j == 0:
                        pe.wait_ge(w_lo, n + 1)
                    if n == CH_BR[0] and j == 0:
                        for br in "ba":
                            for jj in range(4):
                                copied("yT", br, jj)
                    ahi, alo = wview(n)
                    c = slice(P * j, P * j + P)
                    for m, (bhi, blo) in enumerate(((yaT_hi, yaT_lo), (ybT_hi, ybT_lo))):
                        o = opened(*s, m)[:, :]
                        for k in range(4):
                            ins = product(o, ahi[:, 4 * m + k, c], alo[:, 4 * m + k, c], bhi[:, k, :], blo[:, k, :],
                                          k == 0, k == 3)
                        ins.then_inc(full(*s, m), 1)
                elif kind == "cscore":
                    hx = s[1]
                    for n in (CH_CK if hx == 0 else []) + [CH_CQ[hx]]:
                        for j in (0, 1):
                            copied("fm", n, j)
                    for m in (0, 1):
                        o = opened("cscore", hx, m)
                        for a in (0, 1):
                            qt = 2 * m + a
                            for k in (0, 1):
                                ins = pe.matmul(o[:, N_MEM * a:N_MEM * a + N_MEM], qcT[:, 2 * hx + k, P * qt:P * qt + P],
                                                kcT[:, 2 * hx + k, :], start=(k == 0), stop=(k == 1))
                        ins.then_inc(full("cscore", hx, m), 1)
                elif kind == "ctr":
                    hx = s[1]
                    pe.wait_ge(cfin_done, hx + 1)
                    for m in range(MT):
                        o = opened("ctr", hx, m)
                        for qt in range(TT):
                            ins = pe.transpose(o[:, P * qt:P * qt + P], cp[:, hx % 2, qt, P * m:P * m + P], ident[:, :])
                        ins.then_inc(full("ctr", hx, m), 1)
                elif kind == "cav":
                    hx = s[1]
                    if hx == 0:
                        for n, _ in (CH_CV[0], 0), (CH_CV[1], 0):
                            for t in range(MT):
                                copied("tm", n, t)
                    for m in range(MT):
                        copied("ctr", hx, m)
                    for m in (0, 1):
                        o = opened("cav", hx, m)
                        for k in range(MT):
                            ins = pe.matmul(o[:, :], vc[:, k, DH_X * hx + P * m:DH_X * hx + P * m + P], cpT[:, k, :],
                                            start=(k == 0), stop=(k == MT - 1))
                        ins.then_inc(full("cav", hx, m), 1)
                elif kind == "logits":
                    pe.wait_ge(gain_loaded, 16 * 6)
                    for k in range(KT):
                        copied("fT", k)
                    o = opened("logits")
                    for t in range(TT):
                        for k in range(KT):
                            ins = pe.matmul(o[:, (NG + NE) * t:(NG + NE) * (t + 1)], fT[:, k, P * t:P * t + P],
                                            wr[:, k, :], start=(k == 0), stop=(k == KT - 1))
                    ins.then_inc(full("logits"), 1)
                elif kind == "rank":
                    pe.wait_ge(const_done, 2)
                    pe.wait_ge(onehots, 1)
                    o = opened("rank")
                    for t in range(TT + 1):
                        for j in range(min(t + 1, TT)):
                            ins = pe.matmul(o[:, NE * t:NE * t + NE], (tri if j == t else ones)[:, :], M_bf[:, j, :],
                                            start=(j == 0), stop=(j == min(t, TT - 1)))
                    ins.then_inc(full("rank"), 1)

            def transpose_rows(i):
                for k in range(KT):
                    ins = pe.transpose(ps[0][:, BLK * k:BLK * k + BLK], blk[:, P * k:P * k + P], ident[0:BLK, 0:BLK])
                ins.then_inc(xt_done, 1)

            def up(i, c):
                pe.wait_ge(e_wlo, i * 4 + (c + 1))
                for k in range(4):
                    kk = 4 * (c % 2) + k
                    a = Xs[:, kk, :, :].rearrange("p a n -> p (a n)")
                    v = slice(512 * k, 512 * k + 512)
                    pe.matmul(ps[1 + c // 2][:, :], a, whi[c][:, v], start=(kk == 0), stop=False)
                    ins = pe.matmul(ps[1 + c // 2][:, :], a, wlo[c][:, v], start=False, stop=(kk == KT - 1))
                ins.then_inc(e_wused, 1)

            def turn(src, c0):
                for f in range(4):
                    ins = pe.matmul(ps[3][:, c0 + BLK * f:c0 + BLK * f + BLK], src[:, P * f:P * f + P], ii[:, :],
                                    start=True, stop=True)
                return ins

            def down(i, c):
                pe.wait_ge(raw_loaded[c], i * 16 + (E_RAW[c] + 16))
                w = raw_view(c)
                for f in (0, 1):
                    ff = 2 * (c - 4) + f
                    for n in (0, 1):
                        ins = pe.matmul(ps[4 + n][0:BLK, :], HT[:, ff, :], w[:, f, 512 * n:512 * n + 512],
                                        start=(ff == 0), stop=(ff == 3))
                ins.then_inc(w2_used, 1)

            def down_first(i):
                pe.wait_ge(ht_done, i + 2)
                pe.wait_ge(ys_act, i + 1)
                pe.wait_ge(ys_dve, i + 1)
                down(i, 4)

            def body(i, first=False):
                pe.wait_ge(xs_lo, i + 1)
                pe.wait_ge(gs_done, i + 1)
                up(i, 0)
                up(i, 1)
                if not first:
                    down_first(i - 1)
                pe.wait_ge(us_done, i + 1)
                up(i, 2)
                pe.wait_ge(gs_done, i + 2)
                pe.wait_ge(ht_done, i + 1)
                turn(Gs, 0).then_inc(gt_done, 1)
                pe.wait_ge(blk_loaded, i * 16 + 32)
                up(i, 3)
                transpose_rows(i + 1)
                if not first:
                    down(i - 1, 5)
                pe.wait_ge(us_done, i + 2)
                turn(Us, 4 * BLK).then_inc(ut_done, 1)

            for x_ in (e_wused, w2_used, gt_done, ut_done):
                pe.sem_inc(x_, 1)
            for b in range(6):
                pe.wait_ge(bank_free[b], bank_uses[b])
            pe.wait_ge(blk_loaded, 16)
            transpose_rows(0)
            body(0, first=True)
            with pe.Fori(1, NE) as i:
                body(i)
            n_over = pe.value_load(over_i[0:1, 0:1], min_val=0, max_val=MAX_OVER)
            with pe.If(n_over > 0):
                with pe.Fori(NE, n_over + NE) as i:
                    body(i)
            down_first(n_over + (NE - 1))
            down(n_over + (NE - 1), 5)


_INS = ["x", "mem", "mix_norm", "w_in", "lam_q1", "lam_k1", "lam_q2", "lam_k2", "diff_subln", "w_branch_a",
        "w_branch_b", "w_gate", "b_gate", "w_out", "cross_norm", "mem_norm", "w_cq", "w_ckv", "w_co", "ffn_norm",
        "w_group", "b_group", "w_router", "b_router", "w1", "w3", "w2", "final_norm"]


def kernel(**inputs):
    import numpy as np
    import concourse.bacc as bacc
    from concourse.bass_utils import run_bass_kernel_spmd

    nc = bacc.Bacc("TRN2", target_bir_lowering=False, num_devices=1)
    arrays, args = {}, {}
    for name in _INS:
        a = np.ascontiguousarray(inputs[name])
        arrays[f"in_{name}"] = a
        args[name] = nc.dram_tensor(f"in_{name}", a.shape, mybir.dt.from_np(a.dtype), kind="ExternalInput").ap()
    out = nc.dram_tensor("out", (1, SEQ, D), mybir.dt.float32, kind="ExternalOutput").ap()
    build(nc, out=out, **args)
    return run_bass_kernel_spmd(nc, [arrays], core_ids=[0]).results[0]["out"]
```

```python
import math

import concourse.bass as bass
from concourse import mybir

EPS = 1e-6
D = 1024
SEQ = 512
P = 128
KT = D // P
TT = SEQ // P
CHUNK = 64
H_A, DH_A = 4, 64
H_B, DH_B = 8, 64
H_I, D_I = 4, 64
K_SEL = min(256, SEQ // 4)
N_MEM = 256
MT = N_MEM // P
H_X = 4
DH_X = D // H_X
NG, EPG = 4, 8
NE = NG * EPG
DE = 512
BLK = 64
TOPK = 2
MAX_OVER = SEQ * TOPK // (BLK + 1) + 1
N_BLOCKS = -(-(NE + MAX_OVER + 1) // 2) * 2
LAMBDA_INIT = 0.8 - 0.6 * math.exp(-0.3 * 0)
BIG = 1e30
TAKEN = -3e38
NROUND = K_SEL // 8

C_QA, C_KA, C_VA = 0, 512, 1024
C_QB, C_KB, C_VB = 1536, 2048, 2112
C_QI, C_KI, C_WI = 2176, 2432, 2496


def build(nc, x, mem, mix_norm, w_in, lam_q1, lam_k1, lam_q2, lam_k2, diff_subln, w_branch_a, w_branch_b,
          w_gate, b_gate, w_out, cross_norm, mem_norm, w_cq, w_ckv, w_co, ffn_norm, w_group, b_group,
          w_router, b_router, w1, w3, w2, final_norm, out):
    f32, f32r, bf16, i32 = mybir.dt.float32, mybir.dt.float32r, mybir.dt.bfloat16, mybir.dt.int32
    ACT, ALU, AX = mybir.ActivationFunctionType, mybir.AluOpType, mybir.AxisListType

    sbuf_at = [-(-nc.sbuf_base // 32) * 32]

    def region(nbytes):
        start = sbuf_at[0]
        sbuf_at[0] += -(-nbytes // 32) * 32
        return start

    def at(name, shape, dtype, start, offset=0):
        return nc.alloc_sbuf_tensor_at(name, shape, dtype, offset=start + offset)

    KB = 1024
    R_RAW = region(48 * KB)
    R_W = region(32 * KB)
    R_A = region(32 * KB)
    R_B = region(32 * KB)
    R_C = region(41 * KB)
    R_H = region(16 * KB)
    WCH = 2048
    raw = [at(f"raw{s}", [P, WCH], f32, R_RAW, 8 * KB * s) for s in range(6)]
    whi = [at(f"whi{s}", [P, WCH], f32r, R_W, 8 * KB * s) for s in range(2)]
    wlo = [at(f"wlo{s}", [P, WCH], f32r, R_W, 16 * KB + 8 * KB * s) for s in range(2)]
    whi += [at(f"whi{s}", [P, WCH], f32r, R_B, 8 * KB * (s - 2)) for s in (2, 3)]
    wlo += [at(f"wlo{s}", [P, WCH], f32r, R_A, 8 * KB * (s - 2)) for s in (2, 3)]
    xT_hi = at("xT_hi", [P, KT, SEQ], f32r, R_A)
    xT_lo = at("xT_lo", [P, KT, SEQ], f32r, R_A, 16 * KB)
    mg_hi = at("mg_hi", [P, KT, SEQ], f32r, R_A)
    mg_lo = at("mg_lo", [P, KT, SEQ], f32r, R_A, 16 * KB)
    cT_hi = at("cT_hi", [P, KT, SEQ], f32r, R_A)
    cT_lo = at("cT_lo", [P, KT, SEQ], f32r, R_A, 16 * KB)
    xf = at("xf", [P, TT, D], f32, R_A, 16 * KB)
    gates = at("gates", [P, 2 * KT, SEQ], f32, R_B)
    junk_raw = at("junk_raw", [P, D], f32, R_RAW, 44 * KB)
    junk_c = at("junk_c", [P, D], f32, R_C, 36 * KB)
    hn = at("hn", [P, TT, D], f32, R_B)
    qcT = at("qcT", [P, KT, SEQ], f32, R_B)
    oT_lo = at("oT_lo", [P, KT, SEQ], f32r, R_B, 16 * KB)
    vbwi = at("vbwi", [DH_B + H_I, SEQ], f32, R_B)
    qaT = at("qaT", [P, H_A, SEQ], f32, R_C)
    kaT = at("kaT", [P, H_A, SEQ], f32, R_C, 8 * KB)
    va = at("va", [P, TT, 512], f32, R_C, 16 * KB)
    qbT = at("qbT", [P, 4, SEQ], f32, R_C, 24 * KB)
    kbT = at("kbT", [P, SEQ], f32, R_C, 32 * KB)
    kiT = at("kiT", [P, SEQ], f32, R_C, 34 * KB)
    qiT = at("qiT", [P, 2, SEQ], f32, R_C, 36 * KB)
    vb = at("vb", [P, TT, DH_B], f32, R_C, 40 * KB)
    yaT_hi = at("yaT_hi", [P, 4, SEQ], f32r, R_C)
    yaT_lo = at("yaT_lo", [P, 4, SEQ], f32r, R_C, 8 * KB)
    ybT_hi = at("ybT_hi", [P, 4, SEQ], f32r, R_C, 16 * KB)
    ybT_lo = at("ybT_lo", [P, 4, SEQ], f32r, R_C, 24 * KB)
    mrow = at("mrow", [P, MT, D], f32, R_C)
    kcT = at("kcT", [P, KT, N_MEM], f32, R_C, 8 * KB)
    mT_hi = at("mT_hi", [P, KT, N_MEM], f32r, R_C, 16 * KB)
    mT_lo = at("mT_lo", [P, KT, N_MEM], f32r, R_C, 24 * KB)
    vc = at("vc", [P, MT, D], f32, R_C, 32 * KB)
    oT_hi = at("oT_hi", [P, KT, SEQ], f32r, R_C, 16 * KB)
    fT = at("fT", [P, KT, SEQ], f32, R_C, 16 * KB)
    gain_f = at("gain_f", [P, D], f32, R_C)
    gain_o = at("gain_o", [P, D], f32, R_C, 4 * KB)
    RT = 1988
    rt = at("rt", [P, RT], f32, R_C, 8 * KB)
    lgT = at("lgT", [NG + NE, SEQ], f32, R_C, 34 * KB)
    wr = at("wr", [P, KT, NG + NE], f32, R_C, 32 * KB)
    tri = at("tri", [P, P], bf16, R_C, 40 * KB)
    ones = at("ones", [P, P], bf16, R_C, 40 * KB + 256)
    M_bf = at("M_bf", [P, TT, NE], bf16, R_C, 40 * KB + 512)
    xrow = at("xrow", [P, TT, D], f32, R_H)
    ya = at("ya", [P, TT, 512], f32, R_H)
    yb = at("yb", [P, TT, 512], f32, R_H, 8 * KB)
    h = at("h", [P, TT, D], f32, R_H)
    blk = at("blk", [BLK, D], f32, R_C, 16 * KB)
    Xs = at("Xs", [P, KT, 2, BLK], f32r, R_C, 20 * KB)
    Gs = at("Gs", [P, DE], f32, R_C, 24 * KB)
    Us = at("Us", [P, DE], f32, R_C, 26 * KB)
    sg = at("sg", [P, 4, BLK], f32, R_C, 28 * KB)
    ug = at("ug", [P, 4, BLK], f32, R_C, 29 * KB)
    HT = at("HT", [P, 4, BLK], f32, R_C, 30 * KB)
    Ys = at("Ys", [BLK, D], f32, R_C)
    gath = at("gath", [P, TOPK * TT, D], f32, R_B)
    sbuf = [[at(f"s{a}{m}", [P, SEQ], f32, R_RAW, (32, 36, 24)[a] * KB + 2 * KB * m) for m in (0, 1)]
            for a in range(3)]
    pT = [[at(f"pT{a}{m}", [P, TT, P], f32, R_RAW, (40, 28)[a] * KB + 2 * KB * m) for m in (0, 1)]
          for a in (0, 1)]
    cp = at("cp", [P, 2, TT, N_MEM], f32, R_RAW, 32 * KB)
    cpT = at("cpT", [P, MT, SEQ], f32, R_RAW, 40 * KB)
    R_S = region(8 * KB - 1200)
    small_at = [0]

    def small(name, shape, dtype=f32):
        n = 4
        for s in shape[1:]:
            n *= s
        t = at(name, shape, dtype, R_S, small_at[0])
        small_at[0] += -(-n // 32) * 32
        assert small_at[0] <= 8 * KB - 1200, small_at
        return t

    work = [None, small("work1", [P, 256]), at("work2", [P, 384], f32, R_RAW, 44 * KB),
            at("work3", [P, 512], f32, R_RAW, 46 * KB)]
    dist = small("dist", [P, SEQ])
    ident = small("ident", [P, P])
    cols = small("cols", [P, 41])
    ii = small("ii", [P, BLK])
    wi = small("wi", [P, TT, H_I])
    zero = small("zero", [P, 256])
    neglam = small("neglam", [P, 4])
    ss = small("ss", [P, 16])
    rs = small("rs", [P, 16])
    nw = small("nw", [P, 16])
    vv = small("vv", [P, 16])
    sqr = small("sqr", [P, 16])
    nmax = small("nmax", [P, 3, 4])
    ssum = small("ssum", [P, 3, 4])
    rsum = small("rsum", [P, 3, 4])
    top8 = small("top8", [P, 8])
    g12 = small("g12", [P, TOPK, TT])
    slot_i = small("slot_i", [P, TOPK, TT], i32)
    over_i = small("over_i", [P, 1 + MAX_OVER], i32)
    crows = at("crows", [41, P], f32, R_RAW, 32 * KB)
    lamr = at("lamr", [P, 4, DH_A], f32, R_RAW, 34 * KB)
    lamp = at("lamp", [P, 2, DH_A], f32, R_RAW, 36 * KB)

    rt_at = [0]

    def rview(*shape):
        n = 1
        for s in shape:
            n *= s
        v = rt[:, rt_at[0]:rt_at[0] + n]
        rt_at[0] += n
        assert rt_at[0] <= RT
        return v if len(shape) == 1 else v.rearrange("p (a b) -> p a b", b=shape[1])

    rview(64)
    r_iota, r_iotam = rview(NE), rview(NE)
    r_log, r_el, r_tmp = rview(TT, NG + NE), rview(TT, NE), rview(TT, NE)
    r_oh = [rview(TT, NE), rview(TT, NE)]
    r_gmax, r_m1, r_m2, r_least, r_gsum, r_e2, r_d2 = (rview(TT) for _ in range(7))
    r_goh, r_gdif, r_gexp = rview(TT, NG), rview(TT, NG), rview(TT, NG)
    r_rank = rview(TT + 1, NE)
    r_over, r_one, r_end, r_base, r_first, r_rest = (rview(NE) for _ in range(6))
    r_full = rview(SEQ // BLK - 1, NE)
    r_cmp = rview(MAX_OVER, NE)
    r_list = rview(1 + MAX_OVER)

    xslots = nc.dram_tensor("xslots", (N_BLOCKS * BLK, D), f32).ap()
    yslots = nc.dram_tensor("yslots", (N_BLOCKS * BLK, D), f32).ap()

    ps = [nc.alloc_psum_tensor(f"ps{b}", [P, 512], f32) for b in range(8)]

    win = w_in[0].rearrange("(k p) n -> p k n", p=P)
    wg = w_gate[0].rearrange("(k p) n -> p k n", p=P)
    wa = w_branch_a[0].rearrange("(k p) n -> p k n", p=P)
    wb = w_branch_b[0].rearrange("(k p) n -> p k n", p=P)
    wo = w_out[0].rearrange("(k p) n -> p k n", p=P)
    wcq = w_cq[0].rearrange("(k p) n -> p k n", p=P)
    wckv = w_ckv[0].rearrange("(k p) n -> p k n", p=P)
    wco = w_co[0].rearrange("(k p) n -> p k n", p=P)

    chunks = []

    def fm_chunk(src, c0):
        chunks.append((256, [(src[:, :, c0:c0 + 256], 0, KT, 0, 256)]))
        return len(chunks) - 1

    def tm_chunks(src, c0):
        for half in (0, 1):
            chunks.append((512, [(src[:, 4 * half:4 * half + 4, c0:c0 + 512], 0, 4, 0, 512)]))
        return len(chunks) - 2

    chunks.append((128, [(win[:, :, c:c + 64], 0, KT, o, 64) for o, c in ((0, C_KB), (64, C_KI))]))
    CH_K = 0
    CH_QI = fm_chunk(win, C_QI)
    chunks.append((68, [(win[:, :, C_VB:C_VB + 64], 0, KT, 0, 64), (win[:, :, C_WI:C_WI + 4], 0, KT, 64, 4)]))
    CH_VBWI = 2
    CH_QA = [fm_chunk(win, C_QA + 256 * j) for j in (0, 1)]
    CH_KA = [fm_chunk(win, C_KA + 256 * j) for j in (0, 1)]
    CH_VA = tm_chunks(win, C_VA)
    CH_QB = [fm_chunk(win, C_QB + 256 * j) for j in (0, 1)]
    CH_G = [fm_chunk(wg, 256 * j) for j in range(8)]
    CH_BR = []
    for j in range(4):
        chunks.append((256, [(wa[:, :, 256 * j:256 * j + 256], 0, 4, 0, 256),
                             (wb[:, :, 256 * j:256 * j + 256], 4, 8, 0, 256)]))
        CH_BR.append(len(chunks) - 1)
    CH_WO = [tm_chunks(wo, 512 * n) for n in (0, 1)]
    CH_CK = [fm_chunk(wckv, 256 * j) for j in range(4)]
    CH_CV = [tm_chunks(wckv, D + 512 * n) for n in (0, 1)]
    CH_CQ = [fm_chunk(wcq, 256 * j) for j in range(4)]
    CH_CO = [tm_chunks(wco, 512 * n) for n in (0, 1)]
    NCH = len(chunks)
    RING = 3
    raw_dmas = [0] * 6
    raw_need = []
    for n, (_, parts) in enumerate(chunks):
        raw_dmas[n % RING] += len(parts)
        raw_need.append(16 * raw_dmas[n % RING])

    def chunk_cols(n):
        ncol, parts = chunks[n]
        return ncol * max(k1 for _, _, k1, _, _ in parts)

    A_UNITS = [("A", qt, hd) for qt in range(TT) for hd in range(H_A)]
    B_UNITS = [("B", qt, pair) for qt in range(TT) for pair in range(H_B // 2)]
    UNITS = A_UNITS + B_UNITS
    steps = [("norm", "x"), ("cols",), ("split", 0)]
    steps += [("xT", k) for k in range(KT)] + [("split", 1), ("lambda",)]

    def fm(n, js=(0, 1)):
        for j in js:
            steps.append(("fm", n, j))
        if n + 2 < NCH:
            steps.append(("split", n + 2))

    def tm(n, kind, between=()):
        steps.append(("tm", n, kind, 0))
        steps.append(("split", n + 2))
        steps.extend(between)
        steps.append(("tm", n, kind, 1))
        steps.extend([("tmout", n, kind)])
        if n + 3 < NCH:
            steps.append(("split", n + 3))

    fm(CH_K, (0,))
    fm(CH_QI)
    steps.append(("vbwi",))
    steps.append(("vbwiT",))
    steps.append(("split", CH_VBWI + 2))
    selecting = [("index", qt, hd) for qt in range(1, TT) for hd in range(H_I)]
    selecting += [("topk", qt, r) for qt in range(1, TT) for r in range(NROUND)]

    def select(n=2):
        steps.extend(selecting[:n])
        del selecting[:n]

    for n in CH_QA + CH_KA:
        for j in (0, 1):
            steps.append(("fm", n, j))
            if j == 1:
                steps.append(("split", n + 2))
            select(2 if selecting[0][0] == "index" else 3)
    steps += [("score", 0), ("score", 1)]
    tm(CH_VA, "va", between=selecting[:4])
    del selecting[:4]
    select(4)
    steps += [("exp", 0), ("exp", 1), ("score", 2)]
    for n in CH_QB:
        steps.append(("fm", n, 0))
        select(3)
        if n == CH_QB[1]:
            steps.append(("fin", 0))
        steps.append(("fm", n, 1))
        steps.append(("split", n + 2))
        select(3 if n == CH_QB[0] else 1)
    YA_NORM = len(A_UNITS) + 2
    gate_tiles = [(CH_G[g // 2], g % 2) for g in range(2 * KT)]
    for u in range(len(UNITS)):
        steps.append(("tr", u))
        if u + 1 < len(UNITS):
            steps.append(("fin", u + 1))
        if u + 3 < len(UNITS):
            _, qt, _ = UNITS[u + 3]
            assert not any(q <= qt for _, q, _ in selecting) or UNITS[u + 3][0] == "A"
            steps.append(("score", u + 3))
        if u + 2 < len(UNITS):
            steps.append(("exp", u + 2))
        if u % 4 == 0 and u:
            steps.append(("split", CH_G[u // 4 - 1] + 2))
        if u < 2 * len(gate_tiles):
            n, j = gate_tiles[u // 2]
            steps.append(("fm" if u % 2 else "fm_half", n, j))
        steps.append(("av", u))
        select(1)
        if u == YA_NORM:
            steps.append(("yanorm",))
        if YA_NORM + 2 <= u < YA_NORM + 6:
            steps.append(("yT", "a", u - YA_NORM - 2))
    steps += [("yT", "b", j) for j in range(4)] + [("split", CH_G[-1] + 2)] + [("sigmoid", i) for i in range(KT // 2)]
    for n in CH_BR:
        for j in (0, 1):
            steps.append(("merge", n, j))
        steps.append(("split", n + 2))
    steps.append(("norm", "mem"))
    tm(CH_WO[0], "wo0")
    tm(CH_WO[1], "wo1", between=[("mT", k) for k in range(KT // 2)])
    steps += [("mT", k) for k in range(KT // 2, KT)]
    steps.append(("norm", "h1"))
    for n in CH_CK:
        fm(n)
    tm(CH_CV[0], "vc0")
    tm(CH_CV[1], "vc1")
    steps += [("cT", k) for k in range(KT)]
    FIRST_SPLITS = (3, 2, 0, 1)
    fm(CH_CQ[0])
    steps.append(("cscore", 0))
    for hx in range(1, H_X):
        n = CH_CQ[hx]
        steps.append(("fm", n, 0))
        if hx >= 2:
            steps.append(("cav", hx - 2))
        steps += [("cfin", hx - 1), ("fm", n, 1), ("ctr", hx - 1), ("split", n + 2), ("cscore", hx)]
    steps += [("cav", H_X - 2), ("cfin", H_X - 1)]
    n = CH_CO[0]
    steps += [("tm", n, "co0", 0), ("ctr", H_X - 1), ("split", n + 2), ("cav", H_X - 1),
              ("tm", n, "co0", 1), ("tmout", n, "co0"), ("split", n + 3)]
    tm(CH_CO[1], "co1", between=[("first_expert", c) for c in FIRST_SPLITS[:2]])
    steps = [s for s in steps if s[0] != "split" or s[1] < NCH]
    steps += [("norm", "h2"), ("fT", 0, 0), ("fT", 0, 1), ("fT", 1, 0), ("fT", 1, 1), ("logits", 0),
              ("fT", 2, 0), ("fT", 2, 1), ("first_expert", 0), ("logits", 1), ("fT", 3, 0), ("fT", 3, 1),
              ("first_expert", 1), ("logits", 2), ("logits", 3), ("logitsT",), ("rank",)]

    use, fills = {}, [0]

    def fill(*key):
        use[key] = (fills[0] % 8, fills[0] // 8)
        fills[0] += 1

    for s in steps:
        kind = s[0]
        if kind == "fm_half":
            fill("fm", *s[1:])
        elif s in use:
            continue
        elif kind in ("cols", "xT", "mT", "cT", "fT", "fm", "vbwi", "vbwiT", "index", "yT", "logitsT", "rank", "av"):
            fill(*s)
        elif s == ("logits", 0):
            fill("logits")
        elif kind == "tm" and s[3] == 0:
            for t in range(MT if s[2][:2] == "vc" else TT):
                fill("tm", s[1], t)
        elif kind in ("score", "tr"):
            u = UNITS[s[1]]
            for m in range(1 if (kind, u[0]) == ("tr", "A") else 2):
                fill(kind, s[1], m)
        elif kind in ("merge", "cscore", "ctr", "cav"):
            for m in (0, 1):
                fill(*s, m)
    bank_uses = [max([n + 1 for b, n in use.values() if b == bank] or [0]) for bank in range(8)]

    sem = nc.alloc_semaphore
    bank_full = [sem(f"bank_full{b}") for b in range(8)]
    bank_free = [sem(f"bank_free{b}") for b in range(8)]
    raw_loaded = [sem(f"raw_loaded{s}") for s in range(6)]
    w_hi, w_lo, half_used = sem("w_hi"), sem("w_lo"), sem("half_used")
    in_loaded, mem_loaded, h_loaded, gain_loaded = (sem(n) for n in ("in_loaded", "mem_loaded", "h_loaded", "gain_loaded"))
    x_loaded = [sem(f"x_loaded{t}") for t in range(TT)]
    const_done, zeroed, keys_copied = sem("const_done"), sem("zeroed"), sem("keys_copied")
    lam_sum, lam_exp = sem("lam_sum"), sem("lam_exp")
    n_sum, n_mean, n_root, n_out = (sem(n) for n in ("norm_sum", "norm_mean", "norm_root", "norm_out"))
    act_hi = sem("act_hi")
    index_added = sem("index_added")
    max_done, exp_done, fin_done = sem("max_done"), sem("exp_done"), sem("fin_done")
    sig_done, mg_sum, mg_high, mg_low = sem("sig_done"), sem("mg_sum"), sem("mg_high"), sem("mg_low")
    cmax_done, cfin_done = sem("cmax_done"), sem("cfin_done")
    onehots, route_in, route_exp = sem("onehots"), sem("route_in"), sem("route_exp")
    slots_done = sem("slots_done")
    scattered = sem("scattered")
    dve_chain, pool_chain = sem("dve_chain"), sem("pool_chain")
    blk_loaded, xt_done, xs_hi, xs_lo = sem("blk_loaded"), sem("xt_done"), sem("xs_hi"), sem("xs_lo")
    e_whi, e_wlo, e_wused = sem("e_whi"), sem("e_wlo"), sem("e_wused")
    w2_used = sem("w2_used")
    gs_done, us_done, gt_done, ut_done = sem("gs_done"), sem("us_done"), sem("gt_done"), sem("ut_done")
    sg_done, ug_done, ht_done = sem("sg_done"), sem("ug_done"), sem("ht_done")
    ys_act, ys_dve = sem("ys_act"), sem("ys_dve")
    all_stored = sem("all_stored")
    y_stored = sem("y_stored")
    gathered = [sem(f"gathered{b}") for b in range(TOPK * TT)]
    comb_done, out_done = sem("comb_done"), sem("out_done")

    NORMS, SUM_UPTO, OUT_UPTO, NORM_NO = {}, {}, {}, {}
    for name, tiles in (("x", TT), ("ya", 1), ("mem", MT), ("h1", TT), ("h2", TT), ("out", TT)):
        NORM_NO[name] = len(NORMS) + 1 + (TT - 1 if name == "out" else 0)
        NORMS[name] = tiles
        OUT_UPTO[name] = sum(NORMS.values())
        SUM_UPTO[name] = sum(n for a, n in NORMS.items() if a != "ya")
    T_NO = {}
    for s in steps:
        if s[0] in ("xT", "yT", "mT", "cT"):
            T_NO[s] = len(T_NO) + 1

    def kv(qt):
        return P * (qt + 1)

    halves = [s[1] for s in steps if s[0] == "tm" and s[3] == 0]

    def used_when(n):
        if n in halves:
            return half_used, halves.index(n) + 1
        if n - 1 in halves:
            key = ("tm", n - 1, (MT if n - 1 in CH_CV else TT) - 1)
        elif n == CH_VBWI:
            key = ("vbwi",)
        elif n == CH_K:
            key = ("fm", n, 0)
        elif n in CH_BR:
            key = ("merge", n, 1, 1)
        else:
            key = ("fm", n, 1)
        return bank_full[use[key][0]], use[key][1] + 1

    MERGES = [s for s in steps if s[0] == "merge"]
    LAST_CAV = ("cav", H_X - 1, 1)
    E_RAW = [16 * n for n in raw_dmas]

    w1v = w1[0].rearrange("e (k p) n -> e p k n", p=P)
    w3v = w3[0].rearrange("e (k p) n -> e p k n", p=P)
    w2v = w2[0].rearrange("e (k p) n -> e p k n", p=P)

    def expert_src(e, c):
        v = (w1v, w3v, w2v)[c // 2]
        ks = 4 if c < 4 else 2
        if isinstance(e, int):
            return v[e, :, ks * (c % 2):ks * (c % 2) + ks, :]
        return v[bass.ds(e, 1), :, ks * (c % 2):ks * (c % 2) + ks, :].rearrange("e p k n -> (e p) k n")

    def rows_of(slots, i):
        if isinstance(i, int):
            return slots[i * BLK:(i + 1) * BLK, :]
        return slots[bass.ds(i * BLK, BLK), :]

    def raw_view(c):
        return raw[c][:, :].rearrange("p (k n) -> p k n", n=512 if c < 4 else D)

    block = nc.Block()
    with block:

        @block.sync
        def _(sp):
            sp.dma_start(crows[0:8, :], mix_norm[0].rearrange("(k p) -> k p", p=P)).then_inc(in_loaded, 16)
            sp.dma_start(crows[8:16, :], cross_norm[0].rearrange("(k p) -> k p", p=P)).then_inc(in_loaded, 16)
            sp.dma_start(crows[16:24, :], mem_norm[0].rearrange("(k p) -> k p", p=P)).then_inc(in_loaded, 16)
            sp.dma_start(crows[24:40, :], b_gate[0].rearrange("(k p) -> k p", p=P)).then_inc(in_loaded, 16)
            sp.dma_start(crows[40:41, :], diff_subln).then_inc(in_loaded, 16)
            for i, v in enumerate((lam_q1, lam_k1, lam_q2, lam_k2)):
                sp.dma_start(lamr[:, i, :], v[0, :].partition_broadcast(P)).then_inc(in_loaded, 16)

            def load_chunk(n):
                if n >= RING:
                    sp.wait_ge(w_lo, n - RING + 1)
                ncol, parts = chunks[n]
                dst = raw[n % RING][:, 0:chunk_cols(n)].rearrange("p (k n) -> p k n", n=ncol)
                for src, k0, k1, c0, nc_ in parts:
                    sp.dma_start(dst[:, k0:k1, c0:c0 + nc_], src).then_inc(raw_loaded[n % RING], 16)

            for s in steps:
                if s == ("norm", "h2"):
                    b, n = use[LAST_CAV]
                    sp.wait_ge(bank_full[b], n + 1)
                    sp.dma_start(gain_f[:, :], ffn_norm[0, :].partition_broadcast(P)).then_inc(gain_loaded, 16)
                    sp.dma_start(gain_o[:, :], final_norm.partition_broadcast(P)).then_inc(gain_loaded, 16)
                    sp.dma_start(wr[:, :, 0:NG], w_group[0].rearrange("(k p) n -> p k n", p=P)).then_inc(gain_loaded, 16)
                    sp.dma_start(wr[:, :, NG:], w_router[0].rearrange("(k p) n -> p k n", p=P)).then_inc(gain_loaded, 16)
                    sp.dma_start(rt[:, 0:NG], b_group[0, :].partition_broadcast(P)).then_inc(gain_loaded, 16)
                    sp.dma_start(rt[:, NG:NG + NE], b_router[0, :].partition_broadcast(P)).then_inc(gain_loaded, 16)
                elif s == ("norm", "h1"):
                    b, n = use["av", len(UNITS) - 1]
                    sp.wait_ge(bank_full[b], n + 1)
                    sp.dma_start(raw_view(3), expert_src(0, 3)).then_inc(raw_loaded[3], 16)
                elif s[0] == "split":
                    if s[1] == 0:
                        for n in range(RING - 1):
                            load_chunk(n)
                    if s[1] + RING - 1 < NCH:
                        load_chunk(s[1] + RING - 1)
                    elif s[1] == NCH - 1:
                        for n in range(NCH - RING, NCH):
                            sp.wait_ge(w_lo, n + 1)
                            c = n % RING
                            sp.dma_start(raw_view(c), expert_src(0, c)).then_inc(raw_loaded[c], 16)

            for n, c in enumerate(FIRST_SPLITS):
                sp.wait_ge(e_wlo, n + 1)
                sp.dma_start(raw_view(c), expert_src(1, c)).then_inc(raw_loaded[c], 16)
            with sp.Fori(2, NE) as i:
                for c in range(4):
                    sp.wait_ge(e_wlo, i * 4 - 3 + c)
                    sp.dma_start(raw_view(c), expert_src(i, c)).then_inc(raw_loaded[c], 16)
            sp.wait_ge(slots_done, TOPK + 1)
            n_over = sp.value_load(over_i[0:1, 0:1], min_val=0, max_val=MAX_OVER)
            with sp.If(n_over > 0):
                with sp.Fori(NE, n_over + NE) as i:
                    e = sp.value_load(over_i[0:1, bass.ds(i - (NE - 1), 1)], min_val=0, max_val=NE - 1)
                    for c in range(4):
                        sp.wait_ge(e_wlo, i * 4 - 3 + c)
                        sp.dma_start(raw_view(c), expert_src(e, c)).then_inc(raw_loaded[c], 16)
            for t in range(TT):
                sp.wait_ge(n_out, OUT_UPTO["h2"] + t + 1)
                sp.dma_start(out[0, P * t:P * t + P, :], h[:, t, :]).then_inc(out_done, 16)
            sp.wait_ge(out_done, 16 * TT)

        @block.gpsimd
        def _(pool):
            links = [0]

            def link(ins):
                links[0] += 1
                ins.then_inc(pool_chain, 1)
                pool.wait_ge(pool_chain, links[0])

            link(pool.memset(ident[:, :], 0.0))
            link(pool.affine_select(out=ident[:, :], in_=ident[:, :], compare_op=ALU.not_equal, fill=1.0,
                                    base=0, pattern=[[-1, P]], channel_multiplier=1))
            link(pool.memset(ii[:, :], 0.0))
            for base in (0, -BLK):
                link(pool.affine_select(out=ii[:, :], in_=ii[:, :], compare_op=ALU.not_equal, fill=1.0,
                                        base=base, pattern=[[-1, BLK]], channel_multiplier=1))
            link(pool.memset(zero[:, :], 0.0))
            pool.iota(dist[:, :], pattern=[[-1, SEQ]], base=SEQ - P, channel_multiplier=1,
                      allow_small_or_imprecise_dtypes=True).then_inc(const_done, 1)
            pool.wait_ge(raw_loaded[CH_G[2] % RING], raw_need[CH_G[2]])
            pool.dma_start(xslots.rearrange("(p a) (b n) -> p (a b) n", p=P, n=256),
                           zero[:, :].rearrange("p (o n) -> p o n", o=1).to_broadcast([P, N_BLOCKS * BLK * 4 // P, 256])
                           ).then_inc(zeroed, 16)
            pool.dma_start(yslots[NE * BLK:, :].rearrange("(p a) (b n) -> p (a b) n", p=P, n=256),
                           zero[:, :].rearrange("p (o n) -> p o n", o=1).to_broadcast([P, (N_BLOCKS - NE) * BLK * 4 // P, 256])
                           ).then_inc(zeroed, 16)
            b, n = use[("yT", "b", 3)]
            pool.wait_ge(bank_free[b], n + 1)
            pool.dma_start(h[:, :, :], x[0].rearrange("(t p) n -> p t n", p=P)).then_inc(h_loaded, 16)
            pool.wait_ge(mg_low, len(MERGES))
            pool.dma_start(mrow[:, :, :], mem[0].rearrange("(t p) n -> p t n", p=P)).then_inc(mem_loaded, 16)
            b, n = use[LAST_CAV]
            pool.wait_ge(bank_full[b], n + 1)
            for c in (4, 5):
                pool.dma_start(raw_view(c), expert_src(0, c)).then_inc(raw_loaded[c], 16)
            link(pool.memset(ones[:, :], 1.0))
            link(pool.affine_select(out=tri[:, :], in_=ones[:, :], compare_op=ALU.is_gt, fill=0.0,
                                    base=0, pattern=[[1, P]], channel_multiplier=-1))
            pool.iota(rt[:, 64:64 + NE], pattern=[[1, NE]], base=0, channel_multiplier=0,
                      allow_small_or_imprecise_dtypes=True).then_inc(const_done, 1)
            pool.wait_ge(zeroed, 32)
            for k in range(TOPK):
                pool.wait_ge(slots_done, k + 1)
                for t in range(TT):
                    pool.indirect_dma_start(
                        out=xslots, out_offset=bass.IndirectOffsetOnAxis(ap=slot_i[:, k, t:t + 1], axis=0),
                        in_=xf[:, t, :], in_offset=None).then_inc(scattered, 16)
            pool.wait_ge(scattered, 16 * TOPK * TT)
            pool.dma_start(blk[:, :], xslots[0:BLK, :]).then_inc(blk_loaded, 16)

            def body(i, e):
                pool.wait_ge(xt_done, i + 1)
                pool.dma_start(blk[:, :], rows_of(xslots, i + 1)).then_inc(blk_loaded, 16)
                if e is not None:
                    for c in (4, 5):
                        pool.wait_ge(w2_used, i * 2 + (c - 4))
                        pool.dma_start(raw_view(c), expert_src(e, c)).then_inc(raw_loaded[c], 16)

            body(0, None)
            with pool.Fori(1, NE) as i:
                body(i, i)
            n_over = pool.value_load(over_i[0:1, 0:1], min_val=0, max_val=MAX_OVER)
            with pool.If(n_over > 0):
                with pool.Fori(NE, n_over + NE) as i:
                    body(i, pool.value_load(over_i[0:1, bass.ds(i - (NE - 1), 1)], min_val=0, max_val=NE - 1))
            pool.wait_ge(y_stored, n_over * 16 + 16 * (NE + 1))
            pool.sem_inc(all_stored, 1)
            pool.wait_ge(all_stored, 1)
            for t in range(TT):
                for k in range(TOPK):
                    j = TOPK * t + k
                    pool.indirect_dma_start(
                        out=gath[:, j, :], out_offset=None, in_=yslots,
                        in_offset=bass.IndirectOffsetOnAxis(ap=slot_i[:, k, t:t + 1], axis=0)).then_inc(gathered[j], 16)

        @block.scalar
        def _(act):
            def tile_of(*key):
                b, n = use[key]
                act.wait_ge(bank_full[b], n + 1)
                return ps[b]

            def freed(*key):
                return bank_free[use[key][0]]

            def copied(*key):
                b, n = use[key]
                act.wait_ge(bank_free[b], n + 1)

            def root(name, cols_):
                act.wait_ge(n_mean, NORM_NO[name])
                act.activation(sqr[:, 0:cols_], vv[:, 0:cols_], ACT.Sqrt).then_inc(n_root, 1)

            def root_of_tile(name, t):
                act.wait_ge(n_mean, NORM_NO[name] + t)
                act.activation(sqr[:, t:t + 1], vv[:, t:t + 1], ACT.Sqrt).then_inc(n_root, 1)

            def norm(name):
                src = {"x": xrow, "mem": mrow}.get(name, h)
                if name == "mem":
                    act.wait_ge(mem_loaded, 16)
                first = SUM_UPTO[name] - NORMS[name]
                for t in range(NORMS[name]):
                    if first + t:
                        act.wait_ge(n_sum, first + t)
                    if name == "x":
                        act.wait_ge(x_loaded[t], 16)
                    if name in ("h1", "h2"):
                        for n in CH_WO if name == "h1" else CH_CO:
                            copied("tm", n, t)
                    act.activation((junk_c if name == "h2" else junk_raw)[:, :], src[:, t, :], ACT.Square,
                                   accum_out=ss[:, t:t + 1]).then_inc(n_sum, 1)
                    if name == "h2":
                        root_of_tile(name, t)
                if name != "h2":
                    root(name, NORMS[name])

            for t in range(TT):
                act.dma_start(xrow[:, t, :], x[0, P * t:P * t + P, :]).then_inc(x_loaded[t], 16)
            for s in steps:
                kind = s[0]
                if kind == "cols":
                    p = tile_of(*s)
                    act.activation(cols[:, 0:40], p[:, 0:40], ACT.Copy)
                    act.activation(cols[:, 40:41], p[:, 40:41], ACT.Copy, scale=1.0 - LAMBDA_INIT).then_inc(freed(*s), 1)
                elif kind == "lambda":
                    act.wait_ge(lam_sum, 1)
                    act.activation(neglam[:, 0:2], neglam[:, 2:4], ACT.Exp).then_inc(lam_exp, 1)
                elif kind == "norm":
                    norm(s[1])
                elif kind == "split":
                    n = s[1]
                    act.wait_ge(raw_loaded[n % RING], raw_need[n])
                    if n >= 2:
                        act.wait_ge(*used_when(n - 2))
                    w = chunk_cols(n)
                    act.activation(whi[n % 2][:, 0:w], raw[n % RING][:, 0:w], ACT.Copy).then_inc(w_hi, 1)
                elif kind in ("xT", "mT", "cT"):
                    k = s[1]
                    ncol = N_MEM if kind == "mT" else SEQ
                    dst, g0 = {"xT": (xT_hi, 0), "mT": (mT_hi, 16), "cT": (cT_hi, 8)}[kind]
                    p = tile_of(*s)
                    if s == ("xT", 0):
                        copied("cols")
                    act.activation(dst[:, k, :], p[:, 0:ncol], ACT.Copy,
                                   scale=cols[:, g0 + k:g0 + k + 1]).then_inc(act_hi, 1)
                elif kind == "yT":
                    br, j = s[1:]
                    p = tile_of(*s)
                    if br == "a":
                        act.activation(yaT_hi[:, j, :], p[:, :], ACT.Copy, scale=cols[:, 40:41]).then_inc(act_hi, 1)
                    else:
                        act.activation(ybT_hi[:, j, :], p[:, :], ACT.Copy).then_inc(act_hi, 1)
                elif kind == "fT":
                    _, t, half = s
                    act.activation(fT[:, 4 * half:4 * half + 4, P * t:P * t + P],
                                   tile_of(*s)[:, :].rearrange("p (k n) -> p k n", n=P), ACT.Copy).then_inc(freed(*s), 1)
                elif kind == "logitsT":
                    act.activation(lgT[:, :], tile_of("logits")[0:NG + NE, :], ACT.Copy).then_inc(freed("logits"), 1)
                elif kind == "first_expert":
                    c = s[1]
                    act.wait_ge(raw_loaded[c], E_RAW[c] + 16)
                    act.activation(whi[c][:, :], raw[c][:, :], ACT.Copy).then_inc(e_whi, 1)
                elif kind == "fm":
                    n, j = s[1:]
                    p = tile_of(*s)
                    if n == CH_K:
                        lower, upper = slice(0, 64), slice(64, P)
                        act.activation(kbT[lower, :], p[lower, :], ACT.Copy)
                        act.activation(kiT[upper, :], p[upper, :], ACT.Copy).then_inc(freed(*s), 1)
                        copied(*s)
                        act.dma_start(kiT[lower, :], kiT[upper, :]).then_inc(keys_copied, 16)
                        act.dma_start(kbT[upper, :], kbT[lower, :]).then_inc(keys_copied, 16)
                    elif n == CH_QI:
                        act.activation(qiT[:, j, :], p[:, :], ACT.Copy).then_inc(freed(*s), 1)
                    elif n in CH_QA:
                        act.activation(qaT[:, 2 * CH_QA.index(n) + j, :], p[:, :], ACT.Copy,
                                       scale=DH_A ** -0.5).then_inc(freed(*s), 1)
                    elif n in CH_KA:
                        act.activation(kaT[:, 2 * CH_KA.index(n) + j, :], p[:, :], ACT.Copy).then_inc(freed(*s), 1)
                    elif n in CH_QB:
                        act.activation(qbT[:, 2 * CH_QB.index(n) + j, :], p[:, :], ACT.Copy,
                                       scale=DH_B ** -0.5).then_inc(freed(*s), 1)
                    elif n in CH_G:
                        g = 2 * CH_G.index(n) + j
                        act.activation(gates[:, g, :], p[:, :], ACT.Identity,
                                       bias=cols[:, 24 + g:25 + g]).then_inc(freed(*s), 1)
                    elif n in CH_CK:
                        act.activation(kcT[:, 2 * CH_CK.index(n) + j, :], p[:, 0:N_MEM], ACT.Copy).then_inc(freed(*s), 1)
                    elif n in CH_CQ:
                        act.activation(qcT[:, 2 * CH_CQ.index(n) + j, :], p[:, :], ACT.Copy,
                                       scale=DH_X ** -0.5).then_inc(freed(*s), 1)
                elif kind == "vbwi":
                    act.activation(vbwi[:, :], tile_of(*s)[0:DH_B + H_I, :], ACT.Copy).then_inc(freed(*s), 1)
                elif kind == "vbwiT":
                    p = tile_of(*s)[:, 0:TT * 68].rearrange("p (t n) -> p t n", n=68)
                    act.activation(wi[:, :, :], p[:, :, 64:68], ACT.Copy, scale=H_I ** -0.5 * D_I ** -0.5)
                    act.activation(vb[:, :, :], p[:, :, 0:64], ACT.Copy).then_inc(freed(*s), 1)
                elif kind == "tmout" and s[2] in ("va", "vc0", "vc1"):
                    n, what = s[1:]
                    for t in range(MT if what != "va" else TT):
                        p = tile_of("tm", n, t)
                        dst = va[:, t, :] if what == "va" else vc[:, t, 512 * int(what[2]):512 * int(what[2]) + 512]
                        act.activation(dst, p[:, :], ACT.Copy).then_inc(freed("tm", n, t), 1)
                elif kind == "index":
                    qt, hd = s[1:]
                    q = (qt - 1) * H_I + hd
                    p = tile_of(*s)
                    if q >= 2:
                        act.wait_ge(index_added, q - 1)
                    act.activation(sbuf[1][q % 2][:, 0:kv(qt)], p[:, 0:kv(qt)], ACT.Relu).then_inc(freed(*s), 1)
                elif kind == "exp":
                    u = s[1]
                    _, qt, _ = UNITS[u]
                    for m in (0, 1):
                        act.wait_ge(max_done, 2 * u + m + 1)
                        b = sbuf[u % 3][m][:, 0:kv(qt)]
                        act.activation(b, b, ACT.Exp, bias=nmax[:, u % 3, m:m + 1],
                                       accum_out=ssum[:, u % 3, m:m + 1]).then_inc(exp_done, 1)
                elif kind == "tr":
                    u = s[1]
                    br, qt, _ = UNITS[u]
                    for m in range(1 if br == "A" else 2):
                        p = tile_of("tr", u, m)
                        if u >= 2:
                            tile_of("av", u - 2)
                        act.activation(pT[u % 2][m][:, 0:qt + 1, :], p[:, 0:kv(qt)].rearrange("p (s q) -> p s q", q=P),
                                       ACT.Copy).then_inc(freed("tr", u, m), 1)
                elif kind == "av":
                    u = s[1]
                    br, qt, j = UNITS[u]
                    if br == "A":
                        p = tile_of(*s)
                        act.activation(p[:, P:2 * P], p[:, 0:P], ACT.Square, scale=rsum[:, u % 3, 0:1],
                                       accum_out=ss[:, H_A * qt + j:H_A * qt + j + 1])
                        act.activation(ya[:, qt, P * j:P * j + P], tile_of(*s)[:, 0:P], ACT.Copy,
                                       scale=rsum[:, u % 3, 0:1]).then_inc(freed(*s), 1)
                elif kind == "yanorm":
                    root("ya", 16)
                elif kind == "sigmoid":
                    for g in (2 * s[1], KT + 2 * s[1]):
                        v = gates[:, g:g + 2, :].rearrange("p g n -> p (g n)")
                        act.activation(v, v, ACT.Sigmoid).then_inc(sig_done, 1)
                elif kind == "merge":
                    i = MERGES.index(s)
                    act.wait_ge(mg_sum, i + 1)
                    act.activation(mg_hi[:, i, :], gates[:, i, :], ACT.Copy).then_inc(mg_high, 1)
                elif kind == "cscore":
                    hx = s[1]
                    for m in (0, 1):
                        act.wait_ge(cmax_done, 2 * hx + m + 1)
                        for a in (0, 1):
                            qt = 2 * m + a
                            e = act.activation(cp[:, hx % 2, qt, :],
                                               ps[use[("cscore", hx, m)][0]][:, N_MEM * a:N_MEM * a + N_MEM],
                                               ACT.Exp, bias=nmax[:, hx % 2, qt:qt + 1],
                                               accum_out=ssum[:, hx % 2, qt:qt + 1])
                        e.then_inc(freed("cscore", hx, m), 1)
                elif kind == "ctr":
                    hx = s[1]
                    for m in range(MT):
                        p = tile_of("ctr", hx, m)
                        if hx >= 1:
                            tile_of("cav", hx - 1, 1)
                        act.activation(cpT[:, m, :], p[:, :], ACT.Copy).then_inc(freed("ctr", hx, m), 1)
                elif kind == "cav":
                    hx = s[1]
                    for m in (0, 1):
                        act.activation(oT_hi[:, 2 * hx + m, :], tile_of("cav", hx, m)[:, :], ACT.Copy).then_inc(act_hi, 1)
            act.wait_ge(route_in, 1)
            act.activation(r_gexp, r_gdif, ACT.Exp).then_inc(route_exp, 1)
            act.wait_ge(route_in, 2)
            act.activation(r_e2, r_d2, ACT.Exp).then_inc(route_exp, 1)

            def split_hi(i, c):
                act.wait_ge(raw_loaded[c], i * 16 + (E_RAW[c] + 16))
                act.wait_ge(e_wused, i * 4 + (c - 2))
                act.activation(whi[c][:, :], raw[c][:, :], ACT.Copy).then_inc(e_whi, 1)

            def rows_hi(i):
                act.wait_ge(xt_done, i + 1)
                act.wait_ge(e_wused, i * 4 + 1)
                act.activation(Xs[:, :, 0, :], ps[0][:, :].rearrange("p (k n) -> p k n", n=BLK),
                               ACT.Copy).then_inc(xs_hi, 1)

            def output(i):
                act.wait_ge(w2_used, i * 2 + 3)
                act.wait_ge(y_stored, i * 16 + 16)
                act.activation(Ys[:, 0:512], ps[4][0:BLK, :], ACT.Copy).then_inc(ys_act, 1)
                act.wait_ge(ys_act, i + 2)
                act.wait_ge(ys_dve, i + 2)
                act.dma_start(rows_of(yslots, i), Ys[:, :]).then_inc(y_stored, 16)

            def body(i, ahead, first=False):
                if ahead:
                    split_hi(i + 1, 0)
                act.wait_ge(e_wused, i * 4 + 3)
                act.wait_ge(gt_done, i + 1)
                act.activation(Gs[:, :], ps[1][:, :], ACT.Copy).then_inc(gs_done, 1)
                if ahead:
                    split_hi(i + 1, 1)
                act.wait_ge(gt_done, i + 2)
                act.wait_ge(ht_done, i + 1)
                act.activation(sg[:, :, :], ps[3][:, 0:4 * BLK].rearrange("p (f n) -> p f n", n=BLK),
                               ACT.Sigmoid).then_inc(sg_done, 1)
                if ahead:
                    split_hi(i + 1, 2)
                act.wait_ge(e_wused, i * 4 + 5)
                act.wait_ge(ut_done, i + 1)
                act.activation(Us[:, :], ps[2][:, :], ACT.Copy).then_inc(us_done, 1)
                rows_hi(i + 1)
                if ahead:
                    split_hi(i + 1, 3)
                if not first:
                    output(i - 1)

            act.sem_inc(gs_done, 1)
            act.sem_inc(us_done, 1)
            act.sem_inc(ys_act, 1)
            act.sem_inc(y_stored, 16)
            rows_hi(0)
            body(0, True, first=True)
            with act.Fori(1, NE - 1) as i:
                body(i, True)
            body(NE - 1, False)
            n_over = act.value_load(over_i[0:1, 0:1], min_val=0, max_val=MAX_OVER)
            with act.If(n_over > 0):
                with act.Fori(NE, n_over + NE) as i:
                    for c in range(4):
                        split_hi(i, c)
                    body(i, False)
            output(n_over + (NE - 1))
            for t in range(TT):
                act.wait_ge(comb_done, TOPK * (t + 1))
                act.wait_ge(n_sum, SUM_UPTO["h2"] + t)
                act.activation(junk_c[:, :], h[:, t, :], ACT.Square, accum_out=ss[:, t:t + 1]).then_inc(n_sum, 1)
                root_of_tile("out", t)

        @block.vector
        def _(dve):
            links = [0]

            def link(ins):
                links[0] += 1
                ins.then_inc(dve_chain, 1)
                dve.wait_ge(dve_chain, links[0])

            def tile_of(*key):
                b, n = use[key]
                dve.wait_ge(bank_full[b], n + 1)
                return ps[b]

            def freed(*key):
                return bank_free[use[key][0]]

            def copied(*key):
                b, n = use[key]
                dve.wait_ge(bank_free[b], n + 1)

            def inverse_root(name, n, c, step=0):
                v, r, w = vv[:, c], rs[:, c], nw[:, c]
                if name != "x" and step == 0:
                    dve.wait_ge(n_out, OUT_UPTO[name] - NORMS[name])
                dve.tensor_scalar(v, ss[:, c], 1.0 / n, EPS, ALU.mult, ALU.add).then_inc(n_mean, 1)
                dve.wait_ge(n_root, NORM_NO[name] + step)
                link(dve.reciprocal(r, sqr[:, c]))
                link(dve.tensor_tensor(w, r, r, ALU.mult))
                link(dve.tensor_tensor(w, w, v, ALU.mult))
                link(dve.tensor_scalar(w, w, -0.5, 1.5, ALU.mult, ALU.add))
                link(dve.tensor_tensor(r, r, w, ALU.mult))

            def norm(name):
                dve.wait_ge(n_sum, SUM_UPTO[name])
                inverse_root(name, D, slice(0, NORMS[name]))
                for t in range(NORMS[name]):
                    r = rs[:, t:t + 1]
                    if name == "x":
                        ins = dve.tensor_scalar(xrow[:, t, :], xrow[:, t, :], r, None, ALU.mult)
                    elif name == "mem":
                        ins = dve.tensor_scalar(mrow[:, t, :], mrow[:, t, :], r, None, ALU.mult)
                    else:
                        ins = dve.tensor_scalar(hn[:, t, :], h[:, t, :], r, None, ALU.mult)
                    ins.then_inc(n_out, 1)

            def norm_of_tile(name, t):
                dve.wait_ge(n_sum, SUM_UPTO[name] - TT + t + 1)
                inverse_root(name, D, slice(t, t + 1), t)
                dst, gain = (xf, gain_f) if name == "h2" else (h, gain_o)
                dve.scalar_tensor_tensor(dst[:, t, :], h[:, t, :], rs[:, t:t + 1], gain[:, :],
                                         ALU.mult, ALU.mult).then_inc(n_out, 1)

            for s in steps:
                kind = s[0]
                if kind == "norm" and s[1] != "h2":
                    norm(s[1])
                elif kind == "lambda":
                    dve.wait_ge(in_loaded, 16 * 9)
                    link(dve.tensor_tensor(lamp[:, :, :], lamr[:, 0:4:2, :], lamr[:, 1:4:2, :], ALU.mult))
                    dve.tensor_reduce(neglam[:, 2:4], lamp[:, :, :], AX.X, ALU.add).then_inc(lam_sum, 1)
                    dve.wait_ge(const_done, 1)
                    link(dve.scalar_tensor_tensor(dist[:, :], dist[:, :], -1.0, dist[:, :], ALU.mult, ALU.max))
                    link(dve.memset(dist[0:CHUNK, SEQ - CHUNK:SEQ], BIG))
                    dve.wait_ge(lam_exp, 1)
                    link(dve.tensor_tensor(neglam[:, 2:3], neglam[:, 1:2], neglam[:, 0:1], ALU.subtract))
                    link(dve.tensor_scalar(neglam[:, 0:1], neglam[:, 2:3], -LAMBDA_INIT, None, ALU.add))
                elif kind == "split":
                    n = s[1]
                    w = chunk_cols(n)
                    dve.wait_ge(w_hi, n + 1)
                    dve.tensor_tensor(wlo[n % 2][:, 0:w], raw[n % RING][:, 0:w],
                                      whi[n % 2][:, 0:w].bitcast(f32), ALU.subtract).then_inc(w_lo, 1)
                elif kind in ("xT", "mT", "cT"):
                    k = s[1]
                    ncol = N_MEM if kind == "mT" else SEQ
                    lo, hi, g0 = {"xT": (xT_lo, xT_hi, 0), "mT": (mT_lo, mT_hi, 16), "cT": (cT_lo, cT_hi, 8)}[kind]
                    dve.wait_ge(act_hi, T_NO[s])
                    dve.scalar_tensor_tensor(lo[:, k, :], tile_of(*s)[:, 0:ncol], cols[:, g0 + k:g0 + k + 1],
                                             hi[:, k, :].bitcast(f32), ALU.mult, ALU.subtract).then_inc(freed(*s), 1)
                elif kind == "yT":
                    br, j = s[1:]
                    dve.wait_ge(act_hi, T_NO[s])
                    if br == "a":
                        dve.scalar_tensor_tensor(yaT_lo[:, j, :], tile_of(*s)[:, :], cols[:, 40:41],
                                                 yaT_hi[:, j, :].bitcast(f32), ALU.mult, ALU.subtract).then_inc(freed(*s), 1)
                    else:
                        dve.tensor_tensor(ybT_lo[:, j, :], tile_of(*s)[:, :], ybT_hi[:, j, :].bitcast(f32),
                                          ALU.subtract).then_inc(freed(*s), 1)
                elif kind == "index":
                    qt, hd = s[1:]
                    q = (qt - 1) * H_I + hd
                    copied(*s)
                    r, w = sbuf[1][q % 2][:, 0:kv(qt)], work[qt][:, :]
                    if hd == 0:
                        dve.tensor_scalar(w, r, wi[:, qt, hd:hd + 1], None, ALU.mult).then_inc(index_added, 1)
                    else:
                        dve.scalar_tensor_tensor(w, r, wi[:, qt, hd:hd + 1], w, ALU.mult, ALU.add).then_inc(index_added, 1)
                    dve.wait_ge(index_added, q + 1)
                    if hd == H_I - 1:
                        link(dve.memset(work[qt][0:CHUNK, kv(qt) - CHUNK:kv(qt)], -BIG))
                elif kind == "topk":
                    qt, r = s[1:]
                    w = work[qt][:, :]
                    link(dve.max(top8[:, :], w))
                    link(dve.match_replace(w, top8[:, :], w, TAKEN))
                    if r == NROUND - 1:
                        link(dve.tensor_scalar(w, w, TAKEN / 3, BIG, ALU.is_gt, ALU.mult))
                        link(dve.tensor_tensor(w, w, dist[:, SEQ - kv(qt):SEQ], ALU.add))
                elif kind == "score":
                    u = s[1]
                    br, qt, j = UNITS[u]
                    for m in (0, 1):
                        if br == "A" or qt == 0:
                            d = dist[:, SEQ - kv(qt):SEQ]
                        else:
                            d = work[qt][:, :]
                        slope = 2.0 ** (-8.0 * (j + 1) / H_A) if br == "A" else 2.0 ** (-8.0 * (2 * j + m + 1) / H_B)
                        p = tile_of("score", u, m)
                        b = sbuf[u % 3][m][:, 0:kv(qt)]
                        if u >= 3 and m == 0:
                            tile_of("tr", u - 3, 0 if UNITS[u - 3][0] == "A" else 1)
                        dve.scalar_tensor_tensor(b, d, -slope, p[:, 0:kv(qt)], ALU.mult, ALU.add).then_inc(freed("score", u, m), 1)
                        copied("score", u, m)
                        dve.tensor_reduce(nmax[:, u % 3, m:m + 1], b, AX.X, ALU.max, negate=True).then_inc(max_done, 1)
                elif kind == "fin":
                    u = s[1]
                    br, qt, _ = UNITS[u]
                    dve.wait_ge(exp_done, 2 * u + 2)
                    if u >= 3:
                        copied("av", u - 3)
                    if br == "A":
                        link(dve.reciprocal(rsum[:, u % 3, 0:2], ssum[:, u % 3, 0:2]))
                        link(dve.tensor_scalar(rsum[:, u % 3, 2:3], rsum[:, u % 3, 1:2], neglam[:, 0:1],
                                               ssum[:, u % 3, 0:1], ALU.mult, ALU.mult))
                        p0, p1 = (sbuf[u % 3][m][:, 0:kv(qt)] for m in (0, 1))
                        dve.scalar_tensor_tensor(p0, p1, rsum[:, u % 3, 2:3], p0, ALU.mult, ALU.add).then_inc(fin_done, 1)
                    else:
                        dve.reciprocal(rsum[:, u % 3, 0:2], ssum[:, u % 3, 0:2]).then_inc(fin_done, 1)
                        dve.wait_ge(fin_done, u + 1)
                elif kind == "av":
                    u = s[1]
                    br, qt, j = UNITS[u]
                    if br == "B":
                        p = tile_of(*s)[:, 0:2 * DH_B].rearrange("p (m n) -> p m n", m=2)
                        dve.tensor_tensor(yb[:, qt, P * j:P * j + P].rearrange("p (m n) -> p m n", m=2), p,
                                          rsum[:, u % 3, 0:2].unsqueeze(2).to_broadcast([P, 2, DH_B]),
                                          ALU.mult).then_inc(freed(*s), 1)
                elif kind == "yanorm":
                    copied("av", len(A_UNITS) - 1)
                    inverse_root("ya", 2 * DH_A, slice(0, 16))
                    y = ya[:, :, :].rearrange("p t (j n) -> p (t j) n", n=P)
                    dve.tensor_tensor(y, y, rs[:, 0:16].unsqueeze(2).to_broadcast([P, 16, P]), ALU.mult).then_inc(n_out, 1)
                elif kind == "merge":
                    i = MERGES.index(s)
                    dve.wait_ge(sig_done, 2 * (i // 2) + 2)
                    g0, g1 = gates[:, i, :], gates[:, KT + i, :]
                    dve.tensor_tensor(g0, tile_of(*s, 0)[:, :], g0, ALU.mult).then_inc(freed(*s, 0), 1)
                    dve.tensor_tensor(g1, tile_of(*s, 1)[:, :], g1, ALU.mult).then_inc(freed(*s, 1), 1)
                    copied(*s, 0)
                    copied(*s, 1)
                    dve.tensor_tensor(g0, g0, g1, ALU.add).then_inc(mg_sum, 1)
                    dve.wait_ge(mg_high, i + 1)
                    dve.tensor_tensor(mg_lo[:, i, :], g0, mg_hi[:, i, :].bitcast(f32), ALU.subtract).then_inc(mg_low, 1)
                elif kind == "tmout" and s[2][:2] in ("wo", "co"):
                    n, what = s[1:]
                    half = int(what[2])
                    if what == "wo0":
                        dve.wait_ge(h_loaded, 16)
                    for t in range(TT):
                        v = h[:, t, 512 * half:512 * half + 512]
                        dve.tensor_tensor(v, tile_of("tm", n, t)[:, :], v, ALU.add).then_inc(freed("tm", n, t), 1)
                        if what == "co1" and t == 1:
                            dve.wait_ge(gain_loaded, 16 * 6)
                        if what == "co1" and t:
                            norm_of_tile("h2", t - 1)
                    if what == "co1":
                        norm_of_tile("h2", TT - 1)
                elif kind == "cscore":
                    hx = s[1]
                    for m in (0, 1):
                        p = tile_of("cscore", hx, m)[:, :].rearrange("p (a n) -> p a n", a=2)
                        dve.tensor_reduce(nmax[:, hx % 2, 2 * m:2 * m + 2], p, AX.X, ALU.max, negate=True).then_inc(cmax_done, 1)
                elif kind == "cfin":
                    hx = s[1]
                    copied("cscore", hx, 0)
                    copied("cscore", hx, 1)
                    link(dve.reciprocal(rsum[:, hx % 2, 0:TT], ssum[:, hx % 2, 0:TT]))
                    dve.tensor_tensor(cp[:, hx % 2, :, :], cp[:, hx % 2, :, :],
                                      rsum[:, hx % 2, 0:TT].unsqueeze(2).to_broadcast([P, TT, N_MEM]),
                                      ALU.mult).then_inc(cfin_done, 1)
                elif kind == "cav":
                    hx = s[1]
                    for m in (0, 1):
                        dve.wait_ge(act_hi, len(T_NO) + 2 * hx + m + 1)
                        dve.tensor_tensor(oT_lo[:, 2 * hx + m, :], tile_of("cav", hx, m)[:, :],
                                          oT_hi[:, 2 * hx + m, :].bitcast(f32), ALU.subtract).then_inc(freed("cav", hx, m), 1)
                elif kind == "first_expert":
                    c = s[1]
                    dve.wait_ge(e_whi, FIRST_SPLITS.index(c) + 1)
                    dve.tensor_tensor(wlo[c][:, :], raw[c][:, :], whi[c][:, :].bitcast(f32), ALU.subtract).then_inc(e_wlo, 1)

            dve.wait_ge(const_done, 2)
            dve.wait_ge(gain_loaded, 16 * 6)
            link(dve.memset(r_one, 1.0))
            link(dve.tensor_scalar(r_first, r_iota, float(BLK), None, ALU.mult))
            link(dve.tensor_scalar(r_rest, r_iota, -float(BLK), float(BLK * NE - BLK), ALU.mult, ALU.add))
            link(dve.tensor_scalar(r_iotam, r_iota, -99.0, None, ALU.add))
            p = tile_of("logitsT")[:, 0:TT * (NG + NE)].rearrange("p (t n) -> p t n", t=TT)
            dve.tensor_tensor(r_log, p, rt[:, 0:NG + NE].unsqueeze(1).to_broadcast([P, TT, NG + NE]),
                              ALU.add).then_inc(freed("logitsT"), 1)
            copied("logitsT")

            def first_max(values, width, best, onehot, tmp, least):
                wide = [P, TT, width]
                im = r_iotam[:, 0:width].unsqueeze(1).to_broadcast(wide)
                link(dve.tensor_reduce(best, values, AX.X, ALU.max))
                link(dve.tensor_tensor(tmp, values, best.unsqueeze(2).to_broadcast(wide), ALU.is_equal))
                link(dve.tensor_tensor(tmp, tmp, im, ALU.mult))
                link(dve.tensor_reduce(least, tmp, AX.X, ALU.min))
                link(dve.tensor_tensor(onehot, im, least.unsqueeze(2).to_broadcast(wide), ALU.is_equal))

            gl = r_log[:, :, 0:NG]
            first_max(gl, NG, r_gmax, r_goh, r_tmp[:, :, 0:NG], r_least)
            dve.tensor_tensor(r_gdif, gl, r_gmax.unsqueeze(2).to_broadcast([P, TT, NG]), ALU.subtract).then_inc(route_in, 1)
            link(dve.tensor_scalar(r_goh, r_goh, BIG, -BIG, ALU.mult, ALU.add))
            link(dve.tensor_tensor(r_el.rearrange("p t (g e) -> p t g e", g=NG),
                                   r_log[:, :, NG:].rearrange("p t (g e) -> p t g e", g=NG),
                                   r_goh.unsqueeze(3).to_broadcast([P, TT, NG, EPG]), ALU.add))
            first_max(r_el, NE, r_m1, r_oh[0], r_tmp, r_least)
            link(dve.scalar_tensor_tensor(r_el, r_oh[0], -4 * BIG, r_el, ALU.mult, ALU.add))
            first_max(r_el, NE, r_m2, r_oh[1], r_tmp, r_least)
            dve.tensor_tensor(r_d2, r_m2, r_m1, ALU.subtract).then_inc(route_in, 1)
            dve.tensor_tensor(M_bf[:, :, :], r_oh[0], r_oh[1], ALU.add).then_inc(onehots, 1)
            dve.wait_ge(route_exp, 2)
            link(dve.tensor_reduce(r_gsum, r_gexp, AX.X, ALU.add))
            link(dve.scalar_tensor_tensor(r_gsum, r_e2, 1.0, r_gsum, ALU.add, ALU.mult))
            link(dve.reciprocal(g12[:, 0, :], r_gsum))
            link(dve.tensor_tensor(g12[:, 1, :], g12[:, 0, :], r_e2, ALU.mult))
            p = tile_of("rank")[:, 0:(TT + 1) * NE].rearrange("p (t e) -> p t e", e=NE)
            dve.tensor_copy(r_rank, p).then_inc(freed("rank"), 1)
            copied("rank")
            counts = r_rank[:, TT, :]
            wide = [P, SEQ // BLK - 1, NE]
            link(dve.tensor_tensor(r_full, counts.unsqueeze(1).to_broadcast(wide),
                                   r_first[:, 1:SEQ // BLK].unsqueeze(2).to_broadcast(wide), ALU.is_gt))
            link(dve.tensor_reduce(r_over, r_full.rearrange("p k e -> p e k"), AX.X, ALU.add))
            link(dve.tensor_tensor_scan(r_end, r_one, r_over, 0.0, ALU.mult, ALU.add))
            link(dve.tensor_tensor(r_base, r_end, r_over, ALU.subtract))
            link(dve.scalar_tensor_tensor(r_base, r_base, float(BLK), r_rest, ALU.mult, ALU.add))
            rank = r_rank[:, 0:TT, :]
            link(dve.scalar_tensor_tensor(r_tmp, rank, float(BLK), r_base.unsqueeze(1).to_broadcast([P, TT, NE]),
                                          ALU.is_ge, ALU.mult))
            link(dve.tensor_tensor(r_tmp, r_tmp, rank, ALU.add))
            link(dve.tensor_tensor(r_tmp, r_tmp, r_first.unsqueeze(1).to_broadcast([P, TT, NE]), ALU.add))
            for k in range(TOPK):
                link(dve.tensor_tensor(r_oh[k], r_oh[k], r_tmp, ALU.mult))
                link(dve.tensor_reduce(r_least, r_oh[k], AX.X, ALU.add))
                dve.tensor_copy(slot_i[:, k, :], r_least).then_inc(slots_done, 1)
                dve.wait_ge(slots_done, k + 1)
            wide = [P, MAX_OVER, NE]
            link(dve.tensor_tensor(r_cmp, r_end.unsqueeze(1).to_broadcast(wide),
                                   r_iota[:, 0:MAX_OVER].unsqueeze(2).to_broadcast(wide), ALU.is_le))
            link(dve.tensor_reduce(r_list[:, 1:], r_cmp, AX.X, ALU.add))
            link(dve.tensor_scalar(r_list[:, 1:], r_list[:, 1:], float(NE - 1), None, ALU.min))
            link(dve.tensor_copy(r_list[:, 0:1], r_end[:, NE - 1:NE]))
            dve.tensor_copy(over_i[:, :], r_list).then_inc(slots_done, 1)

            def split_lo(i, c):
                dve.wait_ge(e_whi, i * 4 + (c + 1))
                dve.tensor_tensor(wlo[c][:, :], raw[c][:, :], whi[c][:, :].bitcast(f32), ALU.subtract).then_inc(e_wlo, 1)

            def rows_lo(i):
                dve.wait_ge(xs_hi, i + 1)
                dve.tensor_tensor(Xs[:, :, 1, :], ps[0][:, :].rearrange("p (k n) -> p k n", n=BLK),
                                  Xs[:, :, 0, :].bitcast(f32), ALU.subtract).then_inc(xs_lo, 1)

            def output(i):
                dve.wait_ge(w2_used, i * 2 + 3)
                dve.wait_ge(y_stored, i * 16 + 16)
                dve.tensor_copy(Ys[:, 512:1024], ps[5][0:BLK, :]).then_inc(ys_dve, 1)

            def body(i, ahead, first=False):
                if ahead:
                    for c in range(3):
                        split_lo(i + 1, c)
                rows_lo(i + 1)
                if ahead:
                    split_lo(i + 1, 3)
                dve.wait_ge(sg_done, i + 1)
                dve.wait_ge(ut_done, i + 2)
                dve.tensor_tensor(ug[:, :, :], ps[3][:, 4 * BLK:8 * BLK].rearrange("p (f n) -> p f n", n=BLK),
                                  sg[:, :, :], ALU.mult).then_inc(ug_done, 1)
                dve.wait_ge(ug_done, i + 1)
                dve.wait_ge(w2_used, i * 2 + 1)
                dve.tensor_tensor(HT[:, :, :], ps[3][:, 0:4 * BLK].rearrange("p (f n) -> p f n", n=BLK),
                                  ug[:, :, :], ALU.mult).then_inc(ht_done, 1)
                if not first:
                    output(i - 1)

            dve.sem_inc(ht_done, 1)
            dve.sem_inc(ys_dve, 1)
            rows_lo(0)
            body(0, True, first=True)
            with dve.Fori(1, NE - 1) as i:
                body(i, True)
            body(NE - 1, False)
            n_over = dve.value_load(over_i[0:1, 0:1], min_val=0, max_val=MAX_OVER)
            with dve.If(n_over > 0):
                with dve.Fori(NE, n_over + NE) as i:
                    for c in range(4):
                        split_lo(i, c)
                    body(i, False)
            output(n_over + (NE - 1))

            for t in range(TT):
                for k in range(TOPK):
                    j = TOPK * t + k
                    dve.wait_ge(gathered[j], 16)
                    dve.scalar_tensor_tensor(h[:, t, :], gath[:, j, :], g12[:, k, t:t + 1], h[:, t, :],
                                             ALU.mult, ALU.add).then_inc(comb_done, 1)
                    dve.wait_ge(comb_done, j + 1)
                if t:
                    norm_of_tile("out", t - 1)
            norm_of_tile("out", TT - 1)

        @block.tensor
        def _(pe):
            def opened(*key):
                b, n = use[key]
                if n:
                    pe.wait_ge(bank_free[b], n)
                return ps[b]

            def full(*key):
                return bank_full[use[key][0]]

            def copied(*key):
                b, n = use[key]
                pe.wait_ge(bank_free[b], n + 1)

            def product(o, ahi, alo, bhi, blo, start, stop):
                pe.matmul(o, ahi, bhi, start=start, stop=False)
                pe.matmul(o, ahi, blo, start=False, stop=False)
                return pe.matmul(o, alo, bhi, start=False, stop=stop)

            def wview(n):
                ncol = chunks[n][0]
                return (w[n % 2][:, 0:chunk_cols(n)].rearrange("p (k n) -> p k n", n=ncol) for w in (whi, wlo))

            for s in steps:
                kind = s[0]
                if kind == "cols":
                    pe.wait_ge(in_loaded, 16 * 9)
                    pe.wait_ge(const_done, 1)
                    pe.transpose(opened(*s)[:, 0:41], crows[:, :], ident[0:41, 0:41]).then_inc(full(*s), 1)
                elif kind == "fT":
                    _, t, half = s
                    pe.wait_ge(n_out, OUT_UPTO["h1"] + t + 1)
                    o = opened(*s)
                    for k in range(4):
                        kk = 4 * half + k
                        ins = pe.transpose(o[:, P * k:P * k + P], xf[:, t, P * kk:P * kk + P], ident[:, :])
                    ins.then_inc(full(*s), 1)
                elif kind in ("xT", "mT", "cT"):
                    name, src = {"xT": ("x", xrow), "mT": ("mem", mrow), "cT": ("h1", hn)}[kind]
                    k = s[1]
                    if k == 0:
                        pe.wait_ge(n_out, OUT_UPTO[name])
                    o = opened(*s)
                    for t in range(NORMS[name]):
                        ins = pe.transpose(o[:, P * t:P * t + P], src[:, t, P * k:P * k + P], ident[:, :])
                    ins.then_inc(full(*s), 1)
                elif kind == "yT":
                    br, j = s[1:]
                    if s == ("yT", "b", 0):
                        copied("av", len(UNITS) - 1)
                    if s == ("yT", "a", 0):
                        pe.wait_ge(n_out, OUT_UPTO["ya"])
                    o = opened(*s)
                    for t in range(TT):
                        ins = pe.transpose(o[:, P * t:P * t + P], (ya if br == "a" else yb)[:, t, P * j:P * j + P], ident[:, :])
                    ins.then_inc(full(*s), 1)
                elif kind in ("fm", "fm_half"):
                    n, j = s[1:]
                    halved = ("fm_half", n, j) in steps
                    if n in CH_CK:
                        bhi, blo, ncol, src = mT_hi, mT_lo, N_MEM, "mT"
                    elif n in CH_CQ:
                        bhi, blo, ncol, src = cT_hi, cT_lo, SEQ, "cT"
                    else:
                        bhi, blo, ncol, src = xT_hi, xT_lo, SEQ, "xT"
                    if j == 0:
                        pe.wait_ge(w_lo, n + 1)
                    ks = range(KT)
                    if halved:
                        ks = range(KT // 2) if kind == "fm_half" else range(KT // 2, KT)
                    o = (ps[use["fm", n, j][0]] if halved and kind == "fm" else opened("fm", n, j))[:, 0:ncol]
                    ahi, alo = wview(n)
                    c = slice(P * j, P * j + P)
                    for k in ks:
                        if j == 0 and n in (CH_K, CH_CK[0], CH_CQ[0]):
                            copied(src, k)
                        ins = product(o, ahi[:, k, c], alo[:, k, c], bhi[:, k, :], blo[:, k, :], k == 0, k == KT - 1)
                    if kind == "fm":
                        ins.then_inc(full(*s), 1)
                elif kind == "vbwi":
                    pe.wait_ge(w_lo, CH_VBWI + 1)
                    o = opened(*s)
                    ahi, alo = wview(CH_VBWI)
                    for k in range(KT):
                        ins = product(o[0:DH_B + H_I, :], ahi[:, k, :], alo[:, k, :], xT_hi[:, k, :], xT_lo[:, k, :],
                                      k == 0, k == KT - 1)
                    ins.then_inc(full(*s), 1)
                elif kind == "vbwiT":
                    copied("vbwi")
                    o = opened(*s)
                    for t in range(TT):
                        ins = pe.transpose(o[:, 68 * t:68 * t + 68], vbwi[:, P * t:P * t + P],
                                           ident[0:DH_B + H_I, 0:DH_B + H_I])
                    ins.then_inc(full(*s), 1)
                elif kind == "tm":
                    _, n, what, half = s
                    pe.wait_ge(w_lo, n + half + 1)
                    ahi, alo = {"va": (xT_hi, xT_lo), "wo": (mg_hi, mg_lo), "vc": (mT_hi, mT_lo),
                                "co": (oT_hi, oT_lo)}[what[:2]]
                    if what == "wo0":
                        pe.wait_ge(mg_low, 4 * half + 4)
                    if what == "co0":
                        for hx in (2 * half, 2 * half + 1):
                            for m in (0, 1):
                                copied("cav", hx, m)
                    bhi, blo = wview(n + half)
                    for t in range(MT if what[:2] == "vc" else TT):
                        o = opened("tm", n, t) if half == 0 else ps[use[("tm", n, t)][0]]
                        a = slice(P * t, P * t + P)
                        for k in range(4):
                            kk = 4 * half + k
                            ins = product(o[:, :], ahi[:, kk, a], alo[:, kk, a], bhi[:, k, :], blo[:, k, :],
                                          kk == 0, kk == KT - 1)
                        if half == 1:
                            ins.then_inc(full("tm", n, t), 1)
                    if half == 0:
                        ins.then_inc(half_used, 1)
                elif kind == "index":
                    qt, hd = s[1:]
                    if (qt, hd) == (1, 0):
                        pe.wait_ge(keys_copied, 32)
                        for j in (0, 1):
                            copied("fm", CH_QI, j)
                        copied("vbwiT")
                    a = slice(64 * (hd % 2), 64 * (hd % 2) + 64)
                    pe.matmul(opened(*s)[:, 0:kv(qt)], qiT[a, hd // 2, P * qt:P * qt + P], kiT[a, 0:kv(qt)],
                              start=True, stop=True).then_inc(full(*s), 1)
                elif kind == "score":
                    u = s[1]
                    br, qt, j = UNITS[u]
                    if (qt, j) == (0, 0):
                        for n in CH_QA + CH_KA if br == "A" else CH_QB:
                            for jj in (0, 1):
                                copied("fm", n, jj)
                    for m in (0, 1):
                        a = slice(64 * m, 64 * m + 64)
                        q = (qaT if br == "A" else qbT)[a, j, P * qt:P * qt + P]
                        k = kaT[a, j, 0:kv(qt)] if br == "A" else kbT[a, 0:kv(qt)]
                        pe.matmul(opened("score", u, m)[:, 0:kv(qt)], q, k, start=True, stop=True).then_inc(full("score", u, m), 1)
                elif kind == "tr":
                    u = s[1]
                    br, qt, _ = UNITS[u]
                    pe.wait_ge(fin_done, u + 1)
                    for m in range(1 if br == "A" else 2):
                        o = opened("tr", u, m)
                        for k in range(qt + 1):
                            ins = pe.transpose(o[:, P * k:P * k + P], sbuf[u % 3][m][:, P * k:P * k + P], ident[:, :])
                        ins.then_inc(full("tr", u, m), 1)
                elif kind == "av":
                    u = s[1]
                    br, qt, j = UNITS[u]
                    if u == 0:
                        for t in range(TT):
                            copied("tm", CH_VA, t)
                    o = opened(*s)
                    for m in range(1 if br == "A" else 2):
                        copied("tr", u, m)
                        for k in range(qt + 1):
                            v = va[:, k, P * j:P * j + P] if br == "A" else vb[:, k, :]
                            ins = pe.matmul(o[:, DH_B * m:DH_B * m + (P if br == "A" else DH_B)], pT[u % 2][m][:, k, :], v,
                                            start=(k == 0), stop=(k == qt))
                    ins.then_inc(full(*s), 1)
                elif kind == "merge":
                    _, n, j = s
                    if j == 0:
                        pe.wait_ge(w_lo, n + 1)
                    if n == CH_BR[0] and j == 0:
                        for br in "ba":
                            for jj in range(4):
                                copied("yT", br, jj)
                    ahi, alo = wview(n)
                    c = slice(P * j, P * j + P)
                    for m, (bhi, blo) in enumerate(((yaT_hi, yaT_lo), (ybT_hi, ybT_lo))):
                        o = opened(*s, m)[:, :]
                        for k in range(4):
                            ins = product(o, ahi[:, 4 * m + k, c], alo[:, 4 * m + k, c], bhi[:, k, :], blo[:, k, :],
                                          k == 0, k == 3)
                        ins.then_inc(full(*s, m), 1)
                elif kind == "cscore":
                    hx = s[1]
                    for n in (CH_CK if hx == 0 else []) + [CH_CQ[hx]]:
                        for j in (0, 1):
                            copied("fm", n, j)
                    for m in (0, 1):
                        o = opened("cscore", hx, m)
                        for a in (0, 1):
                            qt = 2 * m + a
                            for k in (0, 1):
                                ins = pe.matmul(o[:, N_MEM * a:N_MEM * a + N_MEM], qcT[:, 2 * hx + k, P * qt:P * qt + P],
                                                kcT[:, 2 * hx + k, :], start=(k == 0), stop=(k == 1))
                        ins.then_inc(full("cscore", hx, m), 1)
                elif kind == "ctr":
                    hx = s[1]
                    pe.wait_ge(cfin_done, hx + 1)
                    for m in range(MT):
                        o = opened("ctr", hx, m)
                        for qt in range(TT):
                            ins = pe.transpose(o[:, P * qt:P * qt + P], cp[:, hx % 2, qt, P * m:P * m + P], ident[:, :])
                        ins.then_inc(full("ctr", hx, m), 1)
                elif kind == "cav":
                    hx = s[1]
                    if hx == 0:
                        for n, _ in (CH_CV[0], 0), (CH_CV[1], 0):
                            for t in range(MT):
                                copied("tm", n, t)
                    for m in range(MT):
                        copied("ctr", hx, m)
                    for m in (0, 1):
                        o = opened("cav", hx, m)
                        for k in range(MT):
                            ins = pe.matmul(o[:, :], vc[:, k, DH_X * hx + P * m:DH_X * hx + P * m + P], cpT[:, k, :],
                                            start=(k == 0), stop=(k == MT - 1))
                        ins.then_inc(full("cav", hx, m), 1)
                elif kind == "logits":
                    t = s[1]
                    if t == 0:
                        pe.wait_ge(gain_loaded, 16 * 6)
                    o = opened("logits") if t == 0 else ps[use[("logits",)][0]]
                    for half in (0, 1):
                        copied("fT", t, half)
                    for k in range(KT):
                        ins = pe.matmul(o[0:NG + NE, P * t:P * t + P], wr[:, k, :], fT[:, k, P * t:P * t + P],
                                        start=(k == 0), stop=(k == KT - 1))
                    if t == TT - 1:
                        ins.then_inc(full("logits"), 1)
                elif kind == "logitsT":
                    copied("logits")
                    o = opened("logitsT")
                    for t in range(TT):
                        ins = pe.transpose(o[:, (NG + NE) * t:(NG + NE) * (t + 1)], lgT[:, P * t:P * t + P],
                                           ident[0:NG + NE, 0:NG + NE])
                    ins.then_inc(full("logitsT"), 1)
                elif kind == "rank":
                    pe.wait_ge(const_done, 2)
                    pe.wait_ge(onehots, 1)
                    o = opened("rank")
                    for t in range(TT + 1):
                        for j in range(min(t + 1, TT)):
                            ins = pe.matmul(o[:, NE * t:NE * t + NE], (tri if j == t else ones)[:, :], M_bf[:, j, :],
                                            start=(j == 0), stop=(j == min(t, TT - 1)))
                    ins.then_inc(full("rank"), 1)

            def transpose_rows(i):
                for k in range(KT):
                    ins = pe.transpose(ps[0][:, BLK * k:BLK * k + BLK], blk[:, P * k:P * k + P], ident[0:BLK, 0:BLK])
                ins.then_inc(xt_done, 1)

            def up(i, c):
                pe.wait_ge(e_wlo, i * 4 + (c + 1))
                for k in range(4):
                    kk = 4 * (c % 2) + k
                    a = Xs[:, kk, :, :].rearrange("p a n -> p (a n)")
                    v = slice(512 * k, 512 * k + 512)
                    pe.matmul(ps[1 + c // 2][:, :], a, whi[c][:, v], start=(kk == 0), stop=False)
                    ins = pe.matmul(ps[1 + c // 2][:, :], a, wlo[c][:, v], start=False, stop=(kk == KT - 1))
                ins.then_inc(e_wused, 1)

            def turn(src, c0):
                for f in range(4):
                    ins = pe.matmul(ps[3][:, c0 + BLK * f:c0 + BLK * f + BLK], src[:, P * f:P * f + P], ii[:, :],
                                    start=True, stop=True)
                return ins

            def down(i, c):
                pe.wait_ge(raw_loaded[c], i * 16 + (E_RAW[c] + 16))
                w = raw_view(c)
                for f in (0, 1):
                    ff = 2 * (c - 4) + f
                    for n in (0, 1):
                        ins = pe.matmul(ps[4 + n][0:BLK, :], HT[:, ff, :], w[:, f, 512 * n:512 * n + 512],
                                        start=(ff == 0), stop=(ff == 3))
                ins.then_inc(w2_used, 1)

            def down_first(i):
                pe.wait_ge(ht_done, i + 2)
                pe.wait_ge(ys_act, i + 1)
                pe.wait_ge(ys_dve, i + 1)
                down(i, 4)

            def body(i, first=False):
                pe.wait_ge(xs_lo, i + 1)
                pe.wait_ge(gs_done, i + 1)
                up(i, 0)
                up(i, 1)
                if not first:
                    down_first(i - 1)
                pe.wait_ge(us_done, i + 1)
                up(i, 2)
                pe.wait_ge(gs_done, i + 2)
                pe.wait_ge(ht_done, i + 1)
                turn(Gs, 0).then_inc(gt_done, 1)
                pe.wait_ge(blk_loaded, i * 16 + 32)
                up(i, 3)
                transpose_rows(i + 1)
                if not first:
                    down(i - 1, 5)
                pe.wait_ge(us_done, i + 2)
                turn(Us, 4 * BLK).then_inc(ut_done, 1)

            for x_ in (e_wused, w2_used, gt_done, ut_done):
                pe.sem_inc(x_, 1)
            for b in range(6):
                pe.wait_ge(bank_free[b], bank_uses[b])
            pe.wait_ge(blk_loaded, 16)
            transpose_rows(0)
            pe.wait_ge(e_wlo, 4)
            body(0, first=True)
            with pe.Fori(1, NE) as i:
                body(i)
            n_over = pe.value_load(over_i[0:1, 0:1], min_val=0, max_val=MAX_OVER)
            with pe.If(n_over > 0):
                with pe.Fori(NE, n_over + NE) as i:
                    body(i)
            down_first(n_over + (NE - 1))
            down(n_over + (NE - 1), 5)


_INS = ["x", "mem", "mix_norm", "w_in", "lam_q1", "lam_k1", "lam_q2", "lam_k2", "diff_subln", "w_branch_a",
        "w_branch_b", "w_gate", "b_gate", "w_out", "cross_norm", "mem_norm", "w_cq", "w_ckv", "w_co", "ffn_norm",
        "w_group", "b_group", "w_router", "b_router", "w1", "w3", "w2", "final_norm"]


def kernel(**inputs):
    import numpy as np
    import concourse.bacc as bacc
    from concourse.bass_utils import run_bass_kernel_spmd

    nc = bacc.Bacc("TRN2", target_bir_lowering=False, num_devices=1)
    arrays, args = {}, {}
    for name in _INS:
        a = np.ascontiguousarray(inputs[name])
        arrays[f"in_{name}"] = a
        args[name] = nc.dram_tensor(f"in_{name}", a.shape, mybir.dt.from_np(a.dtype), kind="ExternalInput").ap()
    out = nc.dram_tensor("out", (1, SEQ, D), mybir.dt.float32, kind="ExternalOutput").ap()
    build(nc, out=out, **args)
    return run_bass_kernel_spmd(nc, [arrays], core_ids=[0]).results[0]["out"]
```
